# Optimizing a Trainium2 kernel written in Bass

```python
import math
import jax, jax.numpy as jnp
from jax import lax
import numpy as np

D_MODEL = 1024
BATCH = 1
SEQ = 256
DEPTH = 1

GRID_W = 64
HEAD_DIM = 64
N_HEADS_DIL = 8
N_HEADS_NA = 8
WIDTH_DIL = N_HEADS_DIL * HEAD_DIM
WIDTH_NA = N_HEADS_NA * HEAD_DIM
DIL_PATTERNS = ((128, 1), (512, 4), (2048, 16))
QUERY_BLOCK = 64
NA_ROWS_MAX = 8
NA_COLS = 16
T5_BUCKETS = 32
T5_MAX_DISTANCE = 1024
D_FF = 2816
CONV_WIDTH = 3
RMS_EPS = 1e-6
IN_SPLITS = (WIDTH_DIL, WIDTH_DIL, WIDTH_DIL, WIDTH_NA, WIDTH_NA, WIDTH_NA, D_MODEL, D_MODEL)
IN_COLS = sum(IN_SPLITS)


def rmsnorm(x, g):
    x32 = x.astype(jnp.float32)
    y = x32 * lax.rsqrt(jnp.mean(x32 * x32, axis=-1, keepdims=True) + RMS_EPS)
    return (y * g.astype(jnp.float32)).astype(x.dtype)

def t5_bucket(rel):
    n = T5_BUCKETS // 2
    max_exact = n // 2
    sign_part = jnp.where(rel > 0, n, 0)
    a = jnp.abs(rel)
    af = jnp.maximum(a, 1).astype(jnp.float32)
    large = max_exact + (jnp.log(af / max_exact) / math.log(T5_MAX_DISTANCE / max_exact)
                         * (n - max_exact)).astype(jnp.int32)
    large = jnp.minimum(large, n - 1)
    return sign_part + jnp.where(a < max_exact, a, large)

def dilated_window_attention(q, k, v, rel_bias, window, dilation):
    B, S, H, Dh = q.shape
    L = S // dilation
    R = window // (2 * dilation)
    nb = -(-L // QUERY_BLOCK)
    Lp = nb * QUERY_BLOCK
    KB = QUERY_BLOCK + 2 * R

    def to_res(t):
        return t.reshape(B, L, dilation, H, Dh).transpose(0, 2, 1, 3, 4)

    qr, kr, vr = to_res(q), to_res(k), to_res(v)
    qb = jnp.pad(qr, ((0, 0), (0, 0), (0, Lp - L), (0, 0), (0, 0))).reshape(B, dilation, nb, QUERY_BLOCK, H, Dh)
    pad_kv = ((0, 0), (0, 0), (R, Lp - L + R), (0, 0), (0, 0))
    key_idx = jnp.arange(nb)[:, None] * QUERY_BLOCK + jnp.arange(KB)[None, :]
    kb = jnp.pad(kr, pad_kv)[:, :, key_idx]
    vb = jnp.pad(vr, pad_kv)[:, :, key_idx]

    delta = jnp.arange(KB)[None, :] - jnp.arange(QUERY_BLOCK)[:, None] - R
    key_pos = key_idx - R
    mask = ((key_pos >= 0) & (key_pos < L))[:, None, :] & (jnp.abs(delta) <= R)[None]
    bias = rel_bias[t5_bucket(delta * dilation)].astype(jnp.float32).transpose(2, 0, 1)

    scale = HEAD_DIM ** -0.5
    s = jnp.einsum('bgnqhd,bgnkhd->bghnqk', qb, kb).astype(jnp.float32) * scale + bias[:, None]
    s = jnp.where(mask, s, -jnp.inf)
    m = jnp.max(s, axis=-1, keepdims=True)
    p = jnp.exp(s - m)
    l = jnp.sum(p, axis=-1, keepdims=True)
    o = jnp.einsum('bghnqk,bgnkhd->bgnqhd', (p / l).astype(v.dtype), vb)
    lse = (m + jnp.log(l))[..., 0]

    o = o.reshape(B, dilation, Lp, H, Dh)[:, :, :L].transpose(0, 2, 1, 3, 4).reshape(B, S, H, Dh)
    lse = lse.transpose(0, 1, 3, 4, 2).reshape(B, dilation, Lp, H)[:, :, :L]
    lse = lse.transpose(0, 2, 1, 3).reshape(B, S, H)
    return o, lse

def mixture_of_dilations(q, k, v, rel_bias):
    outs, lses = [], []
    for window, dilation in DIL_PATTERNS:
        o, lse = dilated_window_attention(q, k, v, rel_bias, window, dilation)
        outs.append(o)
        lses.append(lse)
    w = jax.nn.softmax(jnp.stack(lses, axis=0), axis=0)
    return jnp.einsum('gbsh,gbshd->bshd', w.astype(q.dtype), jnp.stack(outs, axis=0))

def neighbourhood_attention_2d(q, k, v, rpb):
    B, S, H, Dh = q.shape
    rows = S // GRID_W
    kh = min(NA_ROWS_MAX, rows)
    q5 = q.reshape(B, rows, GRID_W, H, Dh)
    k5 = k.reshape(B, rows, GRID_W, H, Dh)
    v5 = v.reshape(B, rows, GRID_W, H, Dh)

    r = jnp.arange(rows)
    row_start = jnp.clip(r - kh // 2, 0, rows - kh)
    row_idx = row_start[:, None] + jnp.arange(kh)[None, :]
    kr = k5[:, row_idx]
    vr = v5[:, row_idx]

    cq = jnp.arange(GRID_W)
    col_start = jnp.clip(cq - NA_COLS // 2, 0, GRID_W - NA_COLS)
    col_mask = (cq[None, :] >= col_start[:, None]) & (cq[None, :] < col_start[:, None] + NA_COLS)

    dr = row_idx - r[:, None]
    dc = jnp.clip(cq[None, :] - cq[:, None], -(NA_COLS - 1), NA_COLS - 1)
    bias = rpb.astype(jnp.float32)[:, (dr + NA_ROWS_MAX - 1)[:, :, None, None], (dc + NA_COLS - 1)[None, None]]
    bias = bias.transpose(0, 1, 3, 2, 4)

    scale = HEAD_DIM ** -0.5
    s = jnp.einsum('brqhd,brakhd->bhrqak', q5, kr).astype(jnp.float32) * scale + bias[None]
    s = jnp.where(col_mask[:, None, :], s, -jnp.inf)
    p = jax.nn.softmax(s, axis=(-2, -1))
    o = jnp.einsum('bhrqak,brakhd->brqhd', p.astype(v.dtype), vr)
    return o.reshape(B, S, H, Dh)

def depthwise_conv_seq(u, w, b):
    C = u.shape[-1]
    pad = CONV_WIDTH // 2
    y = lax.conv_general_dilated(u, w.astype(u.dtype)[:, None, :], window_strides=(1,),
                                 padding=((pad, pad),), dimension_numbers=('NWC', 'WIO', 'NWC'),
                                 feature_group_count=C)
    return y + b.astype(u.dtype)

def first_inputs(seed: int = 0) -> dict:
    key = jax.random.key(seed)
    ks = jax.random.split(key, 20)
    f32 = jnp.float32
    nrm = lambda k, shape, s: (jax.random.normal(k, shape, f32) * s)
    return {
        "x": nrm(ks[0], (BATCH, SEQ, D_MODEL), 1.0),
        "c": nrm(ks[1], (BATCH, D_MODEL), 1.0),
        "w_ada": nrm(ks[2], (DEPTH, D_MODEL, 6 * D_MODEL), D_MODEL ** -0.5),
        "b_ada": nrm(ks[3], (DEPTH, 6 * D_MODEL), 0.02),
        "g_mix": 1.0 + nrm(ks[4], (DEPTH, D_MODEL), 0.02),
        "w_in": nrm(ks[5], (DEPTH, D_MODEL, IN_COLS), D_MODEL ** -0.5),
        "rel_bias": nrm(ks[6], (T5_BUCKETS, N_HEADS_DIL), 0.5),
        "na_rpb": nrm(ks[7], (DEPTH, N_HEADS_NA, 2 * NA_ROWS_MAX - 1, 2 * NA_COLS - 1), 0.5),
        "w_branch_dil": nrm(ks[8], (DEPTH, WIDTH_DIL, D_MODEL), WIDTH_DIL ** -0.5),
        "w_branch_na": nrm(ks[9], (DEPTH, WIDTH_NA, D_MODEL), WIDTH_NA ** -0.5),
        "w_out": nrm(ks[10], (DEPTH, D_MODEL, D_MODEL), D_MODEL ** -0.5),
        "g_ffn": 1.0 + nrm(ks[11], (DEPTH, D_MODEL), 0.02),
        "w_up": nrm(ks[12], (DEPTH, D_MODEL, 2 * D_FF), D_MODEL ** -0.5),
        "conv_w": nrm(ks[13], (DEPTH, CONV_WIDTH, 2 * D_FF), CONV_WIDTH ** -0.5),
        "conv_b": nrm(ks[14], (DEPTH, 2 * D_FF), 0.01),
        "w_down": nrm(ks[15], (DEPTH, D_FF, D_MODEL), D_FF ** -0.5),
        "g_final": 1.0 + nrm(ks[16], (D_MODEL,), 0.02),
    }

def first_block(x, c, w_ada, b_ada, g_mix, w_in, rel_bias, na_rpb, w_branch_dil, w_branch_na,
              w_out, g_ffn, w_up, conv_w, conv_b, w_down, g_final):
    B, S, D = x.shape
    split_at = list(np.cumsum(IN_SPLITS)[:-1])
    for i in range(DEPTH):
        ada = jax.nn.silu(c) @ w_ada[i] + b_ada[i]
        shift1, scale1, gate1, shift2, scale2, gate2 = [t[:, None, :] for t in jnp.split(ada, 6, axis=-1)]

        h = rmsnorm(x, g_mix[i]) * (1 + scale1) + shift1
        proj = h @ w_in[i]
        qa, ka, va, qb, kb, vb, ga, gb = jnp.split(proj, split_at, axis=-1)
        heads = lambda t, n: t.reshape(B, S, n, HEAD_DIM)
        oa = mixture_of_dilations(heads(qa, N_HEADS_DIL), heads(ka, N_HEADS_DIL), heads(va, N_HEADS_DIL), rel_bias)
        ob = neighbourhood_attention_2d(heads(qb, N_HEADS_NA), heads(kb, N_HEADS_NA), heads(vb, N_HEADS_NA), na_rpb[i])
        ya = oa.reshape(B, S, WIDTH_DIL) @ w_branch_dil[i]
        yb = ob.reshape(B, S, WIDTH_NA) @ w_branch_na[i]
        merged = jax.nn.sigmoid(ga) * ya + jax.nn.sigmoid(gb) * yb
        x = x + gate1 * (merged @ w_out[i])

        h2 = rmsnorm(x, g_ffn[i]) * (1 + scale2) + shift2
        u = depthwise_conv_seq(h2 @ w_up[i], conv_w[i], conv_b[i])
        u_val, u_gate = jnp.split(u, 2, axis=-1)
        x = x + gate2 * ((jax.nn.gelu(u_gate, approximate=True) * u_val) @ w_down[i])
    return rmsnorm(x, g_final)


DEPTH_2 = 2

MOBA_HEADS = 8
MOBA_BLOCK = 256
MOBA_TOPK = 3
SB_HEADS = 8
MLA_HEADS = 8
MLA_Q_LORA = 256
MLA_KV_LORA = 128
MLA_NOPE = 64
MLA_ROPE = 32
MLA_V = 64
MLA_QK = MLA_NOPE + MLA_ROPE
ROPE_THETA = 500000.0
PARTIAL_ROT = HEAD_DIM // 4
Q_BLOCK = 128
N_BRANCH = 3
BRANCH_W = 512
N_SUB = 3
EPS = 1e-6

MOBA_W = MOBA_HEADS * HEAD_DIM
SB_W = SB_HEADS * HEAD_DIM
SPLIT_1 = 3 * MOBA_W
SPLIT_2 = SPLIT_1 + 3 * SB_W
SPLIT_3 = SPLIT_2 + MLA_Q_LORA
SPLIT_4 = SPLIT_3 + MLA_KV_LORA
SPLIT_5 = SPLIT_4 + MLA_ROPE
N_IN = SPLIT_5 + N_BRANCH * D_MODEL


def rms_norm(x, g):
    xf = x.astype(jnp.float32)
    y = xf * lax.rsqrt(jnp.mean(xf * xf, axis=-1, keepdims=True) + EPS)
    return (y * g.astype(jnp.float32)).astype(x.dtype)

def rope_tables(n_rot, seq):
    inv = jnp.power(jnp.float32(ROPE_THETA), -jnp.arange(0, n_rot, 2, dtype=jnp.float32) / n_rot)
    ang = jnp.arange(seq, dtype=jnp.float32)[:, None] * inv[None, :]
    return jnp.cos(ang), jnp.sin(ang)

def apply_rope(x, cos, sin):
    x1, x2 = jnp.split(x, 2, axis=-1)
    cos = cos.astype(x.dtype)
    sin = sin.astype(x.dtype)
    return jnp.concatenate([x1 * cos - x2 * sin, x1 * sin + x2 * cos], axis=-1)

def partial_rope(x, cos, sin):
    return jnp.concatenate([apply_rope(x[..., :PARTIAL_ROT], cos, sin), x[..., PARTIAL_ROT:]], axis=-1)

def to_heads(x, n_heads):
    b, s, _ = x.shape
    return x.reshape(b, s, n_heads, -1).transpose(0, 2, 1, 3)

def from_heads(x):
    b, h, s, d = x.shape
    return x.transpose(0, 2, 1, 3).reshape(b, s, h * d)

def query_blocks(q):
    b, h, s, d = q.shape
    nq = s // Q_BLOCK
    return q.reshape(b, h, nq, Q_BLOCK, d).transpose(2, 0, 1, 3, 4), nq

def merge_query_blocks(o):
    nq, b, h, qb, d = o.shape
    return o.transpose(1, 2, 0, 3, 4).reshape(b, h, nq * qb, d)

def causal_softmax_attention(q, k, v):
    s_len = k.shape[2]
    scale = q.shape[-1] ** -0.5
    qb, nq = query_blocks(q)
    kpos = jnp.arange(s_len)

    def one(args):
        qc, i = args
        sc = jnp.einsum('bhqd,bhkd->bhqk', qc, k).astype(jnp.float32) * scale
        qpos = i * Q_BLOCK + jnp.arange(Q_BLOCK)
        sc = jnp.where(kpos[None, :] <= qpos[:, None], sc, -jnp.inf)
        p = jax.nn.softmax(sc, axis=-1).astype(v.dtype)
        return jnp.einsum('bhqk,bhkd->bhqd', p, v)

    return merge_query_blocks(lax.map(one, (qb, jnp.arange(nq))))

def stick_breaking_attention(q, k, v):
    s_len = k.shape[2]
    scale = q.shape[-1] ** -0.5
    qb, nq = query_blocks(q)
    kpos = jnp.arange(s_len)

    def one(args):
        qc, i = args
        z = jnp.einsum('bhqd,bhkd->bhqk', qc, k).astype(jnp.float32) * scale
        qpos = i * Q_BLOCK + jnp.arange(Q_BLOCK)
        mask = kpos[None, :] < qpos[:, None]
        log_1m = jnp.where(mask, jax.nn.log_sigmoid(-z), 0.0)
        suffix = lax.cumsum(log_1m, axis=3, reverse=True) - log_1m
        w = jnp.where(mask, jnp.exp(jax.nn.log_sigmoid(z) + suffix), 0.0).astype(v.dtype)
        return jnp.einsum('bhqk,bhkd->bhqd', w, v)

    return merge_query_blocks(lax.map(one, (qb, jnp.arange(nq))))

def moba_attention(q, k, v):
    b, h, s_len, d = q.shape
    n = b * h
    scale = d ** -0.5
    s_pad = -(-s_len // MOBA_BLOCK) * MOBA_BLOCK
    nb = s_pad // MOBA_BLOCK
    top = min(MOBA_TOPK, nb)
    qf = q.reshape(n, s_len, d)
    pad = ((0, 0), (0, s_pad - s_len), (0, 0))
    kb = jnp.pad(k.reshape(n, s_len, d), pad).reshape(n, nb, MOBA_BLOCK, d)
    vb = jnp.pad(v.reshape(n, s_len, d), pad).reshape(n, nb, MOBA_BLOCK, d)
    k_mean = jnp.mean(kb.astype(jnp.float32), axis=2)
    gate = jnp.einsum('nsd,nbd->nsb', qf.astype(jnp.float32), k_mean)
    qblk = jnp.arange(s_len) // MOBA_BLOCK
    past = jnp.arange(nb)[None, :] < qblk[:, None]
    gate = jnp.where(past[None], gate, -jnp.inf)
    _, sel = lax.top_k(gate, top)
    valid = sel < qblk[None, :, None]
    nq = s_len // Q_BLOCK
    q_all = qf.reshape(n, nq, Q_BLOCK, d).transpose(1, 0, 2, 3)
    sel_all = sel.reshape(n, nq, Q_BLOCK, top).transpose(1, 0, 2, 3)
    val_all = valid.reshape(n, nq, Q_BLOCK, top).transpose(1, 0, 2, 3)
    rows = jnp.arange(n)[:, None, None]

    def one(args):
        qc, sc, vc, i = args
        ks = kb[rows, sc]
        vs = vb[rows, sc]
        own = (i * Q_BLOCK) // MOBA_BLOCK
        ko = lax.dynamic_index_in_dim(kb, own, axis=1, keepdims=False)
        vo = lax.dynamic_index_in_dim(vb, own, axis=1, keepdims=False)
        s_sel = jnp.einsum('nqd,nqkjd->nqkj', qc, ks).astype(jnp.float32) * scale
        s_sel = jnp.where(vc[..., None], s_sel, -jnp.inf).reshape(n, Q_BLOCK, top * MOBA_BLOCK)
        s_own = jnp.einsum('nqd,njd->nqj', qc, ko).astype(jnp.float32) * scale
        qpos = i * Q_BLOCK + jnp.arange(Q_BLOCK)
        kpos = own * MOBA_BLOCK + jnp.arange(MOBA_BLOCK)
        s_own = jnp.where(kpos[None, :] <= qpos[:, None], s_own, -jnp.inf)
        p = jax.nn.softmax(jnp.concatenate([s_sel, s_own], axis=-1), axis=-1).astype(v.dtype)
        p_sel = p[..., :top * MOBA_BLOCK].reshape(n, Q_BLOCK, top, MOBA_BLOCK)
        p_own = p[..., top * MOBA_BLOCK:]
        return jnp.einsum('nqkj,nqkjd->nqd', p_sel, vs) + jnp.einsum('nqj,njd->nqd', p_own, vo)

    out = lax.map(one, (q_all, sel_all, val_all, jnp.arange(nq)))
    return out.transpose(1, 0, 2, 3).reshape(b, h, s_len, d)

def token_mixer(hn, w_in, b_gate, q_norm, w_uq, kv_norm, w_ukv, w_branch, w_out, cos_p, sin_p, cos_m, sin_m):
    bsz, s_len, _ = hn.shape
    proj = hn @ w_in
    moba_qkv, sb_qkv, c_q, c_kv, k_rope, gates = jnp.split(
        proj, [SPLIT_1, SPLIT_2, SPLIT_3, SPLIT_4, SPLIT_5], axis=-1)
    qa, ka, va = [to_heads(t, MOBA_HEADS) for t in jnp.split(moba_qkv, 3, axis=-1)]
    y_a = from_heads(moba_attention(partial_rope(qa, cos_p, sin_p), partial_rope(ka, cos_p, sin_p), va))
    qb_, kb_, vb_ = [to_heads(t, SB_HEADS) for t in jnp.split(sb_qkv, 3, axis=-1)]
    y_b = from_heads(stick_breaking_attention(qb_, kb_, vb_))
    qc = to_heads(rms_norm(c_q, q_norm) @ w_uq, MLA_HEADS)
    qc = jnp.concatenate([qc[..., :MLA_NOPE], apply_rope(qc[..., MLA_NOPE:], cos_m, sin_m)], axis=-1)
    kv = to_heads(rms_norm(c_kv, kv_norm) @ w_ukv, MLA_HEADS)
    k_nope, vc = kv[..., :MLA_NOPE], kv[..., MLA_NOPE:]
    kr = jnp.broadcast_to(apply_rope(k_rope, cos_m, sin_m)[:, None], (bsz, MLA_HEADS, s_len, MLA_ROPE))
    y_c = from_heads(causal_softmax_attention(qc, jnp.concatenate([k_nope, kr], axis=-1), vc))
    g = jax.nn.sigmoid(gates.reshape(bsz, s_len, N_BRANCH, D_MODEL) + b_gate)
    ys = jnp.stack([y_a, y_b, y_c], axis=2)
    merged = jnp.einsum('bsnk,nkd,bsnd->bsd', ys, w_branch, g)
    return merged @ w_out

def swiglu(h, w_gate, w_up, w_down):
    return (jax.nn.silu(h @ w_gate) * (h @ w_up)) @ w_down

def modulate(x, g_pre, shift, scale):
    return rms_norm(x, g_pre) * (1 + scale) + shift

def residual_add(x, y, g_post, gate, res_w):
    return x + res_w * (1 + gate) * rms_norm(y, g_post)

def second_inputs(seed: int = 0) -> dict:
    key = jax.random.key(seed)
    ks = jax.random.split(key, 20)
    f32 = jnp.float32
    nrm = lambda k, shape, fan: jax.random.normal(k, shape, f32) * fan ** -0.5
    return {
        'x': jax.random.normal(ks[0], (BATCH, SEQ, D_MODEL), f32),
        'c': jax.random.normal(ks[1], (BATCH, D_MODEL), f32),
        'ada_w': 0.2 * nrm(ks[2], (DEPTH_2, D_MODEL, N_SUB * 3 * D_MODEL), D_MODEL),
        'ada_b': 0.01 * jax.random.normal(ks[3], (DEPTH_2, N_SUB * 3 * D_MODEL), f32),
        'norm_pre': 1.0 + 0.05 * jax.random.normal(ks[4], (DEPTH_2, N_SUB, D_MODEL), f32),
        'norm_post': 1.0 + 0.05 * jax.random.normal(ks[5], (DEPTH_2, N_SUB, D_MODEL), f32),
        'ffn_w_gate': nrm(ks[6], (DEPTH_2, 2, D_MODEL, D_FF), D_MODEL),
        'ffn_w_up': nrm(ks[7], (DEPTH_2, 2, D_MODEL, D_FF), D_MODEL),
        'ffn_w_down': nrm(ks[8], (DEPTH_2, 2, D_FF, D_MODEL), D_FF),
        'mix_w_in': nrm(ks[9], (DEPTH_2, D_MODEL, N_IN), D_MODEL),
        'mix_b_gate': 0.1 * jax.random.normal(ks[10], (DEPTH_2, N_BRANCH, D_MODEL), f32),
        'mla_q_norm': 1.0 + 0.05 * jax.random.normal(ks[11], (DEPTH_2, MLA_Q_LORA), f32),
        'mla_w_uq': nrm(ks[12], (DEPTH_2, MLA_Q_LORA, MLA_HEADS * MLA_QK), MLA_Q_LORA),
        'mla_kv_norm': 1.0 + 0.05 * jax.random.normal(ks[13], (DEPTH_2, MLA_KV_LORA), f32),
        'mla_w_ukv': nrm(ks[14], (DEPTH_2, MLA_KV_LORA, MLA_HEADS * (MLA_NOPE + MLA_V)), MLA_KV_LORA),
        'mix_w_branch': nrm(ks[15], (DEPTH_2, N_BRANCH, BRANCH_W, D_MODEL), BRANCH_W),
        'mix_w_out': nrm(ks[16], (DEPTH_2, D_MODEL, D_MODEL), D_MODEL),
    }

def second_block(x, c, ada_w, ada_b, norm_pre, norm_post, ffn_w_gate, ffn_w_up, ffn_w_down, mix_w_in, mix_b_gate,
              mla_q_norm, mla_w_uq, mla_kv_norm, mla_w_ukv, mix_w_branch, mix_w_out):
    bsz, s_len, _ = x.shape
    cos_p, sin_p = rope_tables(PARTIAL_ROT, s_len)
    cos_m, sin_m = rope_tables(MLA_ROPE, s_len)
    c_act = jax.nn.silu(c)
    for l in range(DEPTH_2):
        mod = (c_act @ ada_w[l] + ada_b[l]).reshape(bsz, N_SUB, 3, D_MODEL)[:, :, :, None, :]
        h = modulate(x, norm_pre[l, 0], mod[:, 0, 0], mod[:, 0, 1])
        x = residual_add(x, swiglu(h, ffn_w_gate[l, 0], ffn_w_up[l, 0], ffn_w_down[l, 0]), norm_post[l, 0], mod[:, 0, 2], 0.5)
        h = modulate(x, norm_pre[l, 1], mod[:, 1, 0], mod[:, 1, 1])
        y = token_mixer(h, mix_w_in[l], mix_b_gate[l], mla_q_norm[l], mla_w_uq[l], mla_kv_norm[l], mla_w_ukv[l],
                        mix_w_branch[l], mix_w_out[l], cos_p, sin_p, cos_m, sin_m)
        x = residual_add(x, y, norm_post[l, 1], mod[:, 1, 2], 1.0)
        h = modulate(x, norm_pre[l, 2], mod[:, 2, 0], mod[:, 2, 1])
        x = residual_add(x, swiglu(h, ffn_w_gate[l, 1], ffn_w_up[l, 1], ffn_w_down[l, 1]), norm_post[l, 2], mod[:, 2, 2], 0.5)
    return x


def setup_inputs(seed=0):
    out = dict(first_inputs(seed))
    for name, value in second_inputs(seed + 1).items():
        if name != "x":
            out[name + "_2"] = value
    return out


def reference(
    x, c, w_ada, b_ada, g_mix, w_in, rel_bias, na_rpb, w_branch_dil, w_branch_na, w_out, g_ffn,
    w_up, conv_w, conv_b, w_down, g_final, c_2, ada_w_2, ada_b_2, norm_pre_2, norm_post_2,
    ffn_w_gate_2, ffn_w_up_2, ffn_w_down_2, mix_w_in_2, mix_b_gate_2, mla_q_norm_2, mla_w_uq_2,
    mla_kv_norm_2, mla_w_ukv_2, mix_w_branch_2, mix_w_out_2,
):
    x = first_block(
        x, c, w_ada, b_ada, g_mix, w_in, rel_bias, na_rpb, w_branch_dil, w_branch_na, w_out,
        g_ffn, w_up, conv_w, conv_b, w_down, g_final,
    )
    return second_block(
        x, c_2, ada_w_2, ada_b_2, norm_pre_2, norm_post_2, ffn_w_gate_2, ffn_w_up_2,
        ffn_w_down_2, mix_w_in_2, mix_b_gate_2, mla_q_norm_2, mla_w_uq_2, mla_kv_norm_2,
        mla_w_ukv_2, mix_w_branch_2, mix_w_out_2,
    )


_drawn_inputs = setup_inputs


def setup_inputs(seed=0):
    import zlib

    import numpy as np

    out = dict(_drawn_inputs(seed))
    spreads = {}
    factors = {'g_mix': 5.625, 'g_ffn': 3.05, 'conv_b': 5.983, 'mla_q_norm_2': 5.852}
    for name, (base, spread) in spreads.items():
        noise = np.random.default_rng([zlib.crc32(name.encode()), seed]).standard_normal(out[name].shape)
        drawn = base * np.exp(spread * noise) if base else spread * noise
        out[name] = __import__('jax').numpy.asarray(drawn.astype(out[name].dtype))
    for name, factor in factors.items():
        out[name] = (out[name] * factor).astype(out[name].dtype)
    return out
```

```python
from contextlib import ExitStack, contextmanager

import numpy as np

import concourse.bass as bass
from concourse import mybir

F32 = mybir.dt.float32
F32R = mybir.dt.float32r
ACT = mybir.ActivationFunctionType
ALU = mybir.AluOpType

P = 128
SEQ = 256
D = 1024
KT = D // P
HEADS = 8
HD = 64
D_FF = 2816
FT = D_FF // P
GRID_W = 64
ROWS = SEQ // GRID_W
LAYERS = 2
MLA_QK = 96
MLA_NOPE = 64
MLA_ROPE = 32
EPS = 1e-6
MASKED = -1e30
CH = 16 * P
RAW = 4
SPLIT = 2
N_RPB = 15 * 31

ONCE = [("start", 0), ("ada", 0), ("norm1", 0), ("dil_qkv", 6), ("dil_attn", 0), ("na_qkv", 6),
        ("na_attn", 0), ("gates1", 8), ("branch1", 4), ("mods1", 0), ("out1", 4), ("norm2", 0),
        ("up1", FT), ("down1", FT // 2), ("norm3", 0)]
LAYER = [("ada0", 0), ("pre0", 0), ("gateup0", FT), ("down0", FT // 2), ("post0", 0),
         ("pre1", 0), ("moba_qkv", 6), ("moba_attn", 0), ("sb_qkv", 6), ("sb_attn", 0),
         ("latent", 2), ("mla_up", 2), ("mla_attn", 0), ("gates", 12), ("branch", 6), ("out", 4),
         ("pre2", 0), ("gateup2", FT), ("down2", FT // 2), ("post2", 0)]
STAGES = ONCE + LAYER + [("end", 0)]
FIRST_CHUNK = {}
_at = 0
for _name, _n in STAGES:
    FIRST_CHUNK[_name] = _at
    _at += _n
ONCE_CHUNKS = sum(n for _, n in ONCE)
LAYER_CHUNKS = sum(n for _, n in LAYER)
assert LAYER_CHUNKS % RAW == 0
CHUNKS = ONCE_CHUNKS + LAYERS * LAYER_CHUNKS
ADA_ONCE = 24
ADA_LAYER = 36
ADA_CHUNKS = ADA_ONCE + LAYERS * ADA_LAYER

def columns(*parts):
    at, out = 0, {}
    for name, n in parts:
        out[name] = slice(at, at + n)
        at += n
    return out, at


PCOL, NPCOL = columns(("c", 8), ("c_2", 8), ("b_ada", 48), ("g_mix", 8), ("g_ffn", 8), ("g_final", 8),
                      ("conv", 8 * FT), ("rel_bias", 8))
LCOL, NLCOL = columns(("ada_b", 72), ("norm_pre", 24), ("norm_post", 24), ("b_gate", 24),
                      ("q_norm", 2), ("kv_norm", 1))
CCOL, NCCOL = columns(("ident", P), ("ones", P), ("causal", 2 * SEQ))
BCOL, NBCOL = columns(("flip", P), ("dil", 2 * SEQ), ("na", 2 * SEQ), ("onehot", 2 * SEQ))
DCOL, NDCOL = columns(("neg_tri", P), ("neg_ones", P), ("rot_p", P), ("rot_m", P), ("cos_p", SEQ),
                      ("sin_p", SEQ), ("cos_m", SEQ), ("sin_m", SEQ), ("sb_add", 2 * SEQ),
                      ("sb_mul", 2 * SEQ))


class Signals:

    def __init__(self, nc, ctx, totals):
        self.nc, self.ctx = nc, ctx
        self.names = {}
        self.totals = totals
        self.seen = {}

    def make(self, name):
        sem = self.ctx.enter_context(self.nc.semaphore(name))
        self.names[id(sem)] = name
        return sem

    def base(self, name, stage, l):
        total = 0
        for s, _ in ONCE:
            if s == stage:
                return total
            total += self.totals.get((s, name), 0)
        round_ = sum(self.totals.get((s, name), 0) for s, _ in LAYER)
        for s, _ in LAYER:
            if s == stage:
                return total + l * round_
            total += self.totals.get((s, name), 0)
        return total + (LAYERS - 1) * round_


class Engine:

    def __init__(self, eng, ops, signals):
        self.eng, self.ops, self.s = eng, ops, signals
        self.stage, self.l, self.times = "start", 0, 1

    def at(self, stage):
        self.stage = stage

    def past(self, sem):
        return self.s.base(self.s.names[id(sem)], self.stage, self.l)

    def adds(self, sem, n=1):
        key = self.stage, self.s.names[id(sem)]
        self.s.seen[key] = self.s.seen.get(key, 0) + n * self.times
        return n

    def in_layers(self):
        return not isinstance(self.l, int)

    @contextmanager
    def loop(self, n):
        self.times *= n
        if self.in_layers():
            self.eng.sem_inc(self.s.passed, 1)
        with self.eng.Fori(0, n) as i:
            yield i
        self.times //= n

    @contextmanager
    def layers(self):
        with self.eng.Fori(0, LAYERS) as l:
            self.l = l
            yield l
        self.l = LAYERS - 1

    def chunk(self, k):
        c = FIRST_CHUNK[self.stage] + k
        return c if self.stage in dict(ONCE) else self.l * LAYER_CHUNKS + c

    def round(self, k0, turn):
        c = (FIRST_CHUNK[self.stage] + k0) // RAW + turn
        return c if self.stage in dict(ONCE) else self.l * (LAYER_CHUNKS // RAW) + c

    def chunks(self, body, head=0):
        n = dict(STAGES)[self.stage]
        for k in range(head):
            body(k, k, 0)
        turns = (n - head) // RAW
        k = head
        if turns > 1:
            with self.loop(turns) as i:
                for j in range(RAW):
                    body(RAW * i + (head + j), head + j, i)
            k = head + RAW * turns
        while k < n:
            body(k, k, 0)
            k += 1

    def slot(self, k0):
        return (FIRST_CHUNK[self.stage] + k0) % RAW


def program(nc, d, totals):
    with ExitStack() as ctx:
        def sb(name, shape, dt=F32, scope=ctx):
            return scope.enter_context(nc.sbuf_tensor(name, shape, dt))

        raw = sb("raw", [P, RAW, CH])
        hi = [sb(f"hi{i}", [P, CH], F32R) for i in range(SPLIT)]
        lo = [sb(f"lo{i}", [P, CH], F32R) for i in range(SPLIT)]
        ada_w = [sb(f"ada_w{i}", [P, CH]) for i in range(2)]
        x = sb("x", [P, KT, SEQ])
        h_hi = sb("h_hi", [P, KT, SEQ], F32R)
        h_lo = sb("h_lo", [P, KT, SEQ], F32R)
        work = [sb(f"work{i}", [P, 2, SEQ]) for i in range(4)]
        rs = sb("rs", [P, 2, SEQ])
        par = sb("par", [P, NPCOL])
        lpar = sb("lpar", [P, NLCOL])
        con = sb("con", [P, NCCOL])
        cs = sb("cs", [P, 16])
        mod = sb("mod", [P, 72])
        gain = sb("gain", [P, 24])
        post_gain = sb("post_gain", [P, 24])
        eps = sb("eps", [P, 1])
        mx = sb("mx", [P, 2, 2])
        neg_mx = sb("neg_mx", [P, 2, 2])
        den = sb("den", [P, 2, 2])
        rden = sb("rden", [P, 2, 2])

        with ExitStack() as scope:
            act_hi = sb("act_hi", [P, FT, SEQ], F32R, scope)
            act_lo = sb("act_lo", [P, FT, SEQ], F32R, scope)
        with ExitStack() as scope:
            flat = sb("flat", [P, KT, SEQ], F32, scope)
        with ExitStack() as scope:
            qm = sb("qm", [P, HEADS, SEQ], F32, scope)
            km = sb("km", [P, HEADS, SEQ], F32, scope)
            v = sb("v", [P, 2, 512], F32, scope)
            br_hi = sb("br_hi", [P, 12, SEQ], F32R, scope)
            br_lo = sb("br_lo", [P, 12, SEQ], F32R, scope)
            gates = sb("gates", [P, 24, SEQ], F32, scope)
            lat_hi = sb("lat_hi", [P, 3, SEQ], F32R, scope)
            lat_lo = sb("lat_lo", [P, 3, SEQ], F32R, scope)
            dcon = sb("dcon", [P, NDCOL], F32, scope)
        with ExitStack() as scope:
            sb("below", [P, (2 * HEADS + 4 + 2 * 12 + 16) * SEQ], F32, scope)
            bcon = sb("bcon", [P, NBCOL], F32, scope)
            rel_tab = sb("rel_tab", [HEADS, 2 * SEQ], F32, scope)
            bias = [sb(f"bias{i}", [P, 2, SEQ], F32, scope) for i in range(2)]
        qt = qm[:, 0:4, :]
        kt_ = km[:, 0:4, :]

        lin = ctx.enter_context(nc.psum_tensor("lin", [P, 4, 512], F32))
        norm_ps = ctx.enter_context(nc.psum_tensor("norm_ps", [P, 512], F32))
        ada_ps = ctx.enter_context(nc.psum_tensor("ada_ps", [P, 512], F32))
        aux = ctx.enter_context(nc.psum_tensor("aux", [P, 2, 512], F32))

        S = Signals(nc, ctx, totals)
        s_passed = S.passed = S.make("passed")
        s_params_in = S.make("params_in")
        s_lpar_in = S.make("lpar_in")
        s_bcon_in = S.make("bcon_in")
        s_dcon_in = S.make("dcon_in")
        s_x_in = S.make("x_in")
        s_rel_stored = S.make("rel_stored")
        s_hi_made = S.make("hi_made")
        s_lo_made = S.make("lo_made")
        s_mm_done = S.make("mm_done")
        s_evac = S.make("evac")
        s_ada_used = S.make("ada_used")
        s_silu_made = S.make("silu_made")
        s_eps_made = S.make("eps_made")
        s_rel_made = S.make("rel_made")
        s_mods_made = S.make("mods_made")
        s_squared = S.make("squared")
        s_summed = S.make("summed")
        s_r_made = S.make("r_made")
        s_flat_made = S.make("flat_made")
        s_h_hi_made = S.make("h_hi_made")
        s_h_ready = S.make("h_ready")
        s_x_made = S.make("x_made")
        s_gated = S.make("gated")
        s_conved = S.make("conved")
        s_taps_made = S.make("taps_made")
        s_act_made = S.make("act_made")
        s_y_made = S.make("y_made")
        s_evac_y = S.make("evac_y")
        s_scored = S.make("scored")
        s_maxed = S.make("maxed")
        s_exped = S.make("exped")
        s_normed = S.make("normed")
        s_transposed = S.make("transposed")
        s_pt_copied = S.make("pt_copied")
        s_pv_done = S.make("pv_done")
        s_o_hi_made = S.make("o_hi_made")
        s_o_taken = S.make("o_taken")
        s_qkv_made = S.make("qkv_made")
        s_turned_in = S.make("turned_in")
        s_turned = S.make("turned")
        s_logged = S.make("logged")
        s_sp_made = S.make("sp_made")
        s_suffixed = S.make("suffixed")
        s_d_made = S.make("d_made")
        s_w_made = S.make("w_made")
        s_lat_made = S.make("lat_made")
        s_lat_hi_made = S.make("lat_hi_made")
        s_lat_ready = S.make("lat_ready")
        s_q_turn = S.make("q_turn")
        s_q_turned = S.make("q_turned")
        s_merged = S.make("merged")
        s_merged_hi = S.make("merged_hi")
        s_out_done = S.make("out_done")
        arrived = [ctx.enter_context(nc.semaphore(f"arrived{i}")) for i in range(RAW)]
        ada_in = [ctx.enter_context(nc.semaphore(f"ada_in{i}")) for i in range(2)]
        bias_in = [ctx.enter_context(nc.semaphore(f"bias_in{i}")) for i in range(2)]

        ident = con[:, CCOL["ident"]]
        ones = con[:, CCOL["ones"]]

        def two(ap):
            return ap.rearrange("p (a t) -> p a t", a=2)

        def over(ap, n):
            return ap.unsqueeze(1).to_broadcast([ap.shape[0], n, ap.shape[1]])

        block = ctx.enter_context(nc.Block())

        @block.sync
        def _(eng):
            e = Engine(eng, nc.sync, S)
            eng.dma_start(par[:], d["par"]).then_inc(s_params_in, e.adds(s_params_in, 16))
            eng.dma_start(con[:], d["con"]).then_inc(s_params_in, e.adds(s_params_in, 16))
            eng.dma_start(x[:], d["x"]).then_inc(s_x_in, e.adds(s_x_in, 16))
            eng.dma_start(bcon[:], d["bcon"]).then_inc(s_bcon_in, e.adds(s_bcon_in, 16))
            for c in range(RAW):
                eng.dma_start(raw[:, c, :], d["w"][c]).then_inc(arrived[c], 16)

            eng.dma_start(dcon[:], d["dcon"]).then_inc(s_dcon_in, e.adds(s_dcon_in, 16))

            def load(c, slot):
                eng.wait_ge(s_lo_made, c - (RAW - 1))
                eng.dma_start(raw[:, slot, :], d["w"][bass.ds(c, 1)].rearrange("o p n -> (o p) n")
                              ).then_inc(arrived[slot], 16)

            turns = (CHUNKS + 1 - RAW) // RAW
            with eng.Fori(0, turns) as i:
                for s in range(RAW):
                    load(RAW * i + (RAW + s), s)
            for c in range(RAW + RAW * turns, CHUNKS + 1):
                load(c, c % RAW)
            e.at("end")
            eng.wait_ge(s_x_made, e.past(s_x_made))
            eng.dma_start(d["out"], x[:]).then_inc(s_out_done, e.adds(s_out_done, 16))
            eng.wait_ge(s_out_done, e.past(s_out_done) + 16)

        @block.gpsimd
        def _(eng):
            e = Engine(eng, nc.gpsimd, S)
            nc.gpsimd.memset(eps[:], EPS).then_inc(s_eps_made, e.adds(s_eps_made))

            def load(a, slot):
                eng.dma_start(ada_w[slot][:], d["ada"][bass.ds(a, 1)].rearrange("o p n -> (o p) n")
                              ).then_inc(ada_in[slot], 16)

            for a in range(2):
                eng.dma_start(ada_w[a][:], d["ada"][a]).then_inc(ada_in[a], 16)
            with eng.Fori(0, ADA_CHUNKS // 2 - 1) as i:
                for s in range(2):
                    eng.wait_ge(s_ada_used, 2 * i + (s + 1))
                    load(2 * i + (s + 2), s)

        @block.tensor
        def _(eng):
            e = Engine(eng, nc.tensor, S)
            mm = nc.tensor.matmul

            def three(out, w_hi, w_lo, a_hi, a_lo, start, stop, skip=False):
                mm(out, w_hi, a_hi, start=start, stop=False, skip_group_check=skip)
                mm(out, w_hi, a_lo, start=False, stop=False, skip_group_check=skip)
                return mm(out, w_lo, a_hi, start=False, stop=stop, skip_group_check=skip)

            def ada_chunk(a, slot, turn, col):
                eng.wait_ge(ada_in[slot], 16 * (turn + 1))
                for j in range(2):
                    for k in range(KT):
                        b = j * KT + k
                        out = ada_ps[:, bass.ds(col + j, 1)] if not isinstance(col, int) \
                            else ada_ps[:, col + j:col + j + 1]
                        ins = mm(out, ada_w[slot][:, b * P:(b + 1) * P],
                                 cs[:, a + k:a + k + 1], start=(k == 0), stop=(k == KT - 1))
                ins.then_inc(s_ada_used, e.adds(s_ada_used))

            def ada_once(a):
                ada_chunk(0, a % 2, a // 2, 2 * a)

            def ada_layer(a, a0, turn2):
                first = (ADA_ONCE // 2) + (ADA_LAYER // 2) * e.l
                ada_chunk(8, a0 % 2, first + a0 // 2 + turn2, 2 * a)

            def fm(k, k0, turn, a_hi=h_hi, a_lo=h_lo, bank=None):
                c = e.chunk(k)
                s = e.slot(k0) % SPLIT
                if not (isinstance(k, int) and k < 2):
                    eng.wait_ge(s_evac, e.past(s_evac) + k - 1)
                eng.wait_ge(s_lo_made, c + 1)
                for j in range(2):
                    for t in range(KT):
                        b = slice((j * KT + t) * P, (j * KT + t + 1) * P)
                        ins = three(lin[:, k0 % 2, j * SEQ:(j + 1) * SEQ], hi[s][:, b], lo[s][:, b],
                                    a_hi[:, t, :], a_lo[:, t, :], t == 0, t == KT - 1)
                ins.then_inc(s_mm_done, e.adds(s_mm_done))

            def tm(k):
                s = e.slot(k) % SPLIT
                eng.wait_ge(s_evac, e.past(s_evac) + k - 1)
                eng.wait_ge(s_lo_made, e.chunk(k) + 1)
                for j in range(2):
                    for t in range(KT):
                        b = slice(t * SEQ, (t + 1) * SEQ)
                        ins = three(lin[:, k % 2, j * SEQ:(j + 1) * SEQ],
                                    h_hi[:, t, j * P:(j + 1) * P], h_lo[:, t, j * P:(j + 1) * P],
                                    hi[s][:, b], lo[s][:, b], t == 0, t == KT - 1)
                ins.then_inc(s_mm_done, e.adds(s_mm_done))

            def enter(stage):
                e.at(stage)
                eng.wait_ge(s_evac, e.past(s_evac))
                eng.wait_ge(s_evac_y, e.past(s_evac_y))
                eng.wait_ge(s_o_taken, e.past(s_o_taken))

            def sums(stage, n=4):
                e.at(stage)
                for p in range(n):
                    eng.wait_ge(s_squared, e.past(s_squared) + p + 1)
                    for j in range(2):
                        ins = mm(norm_ps[:, 0:SEQ], ones, work[p][:, j, :],
                                 start=(p == 0 and j == 0), stop=(p == n - 1 and j == 1))
                ins.then_inc(s_summed, e.adds(s_summed))

            def down(stage):
                enter(stage)
                eng.wait_ge(s_act_made, e.past(s_act_made))

                def body(k, k0, turn):
                    s = e.slot(k0) % SPLIT
                    eng.wait_ge(s_lo_made, e.chunk(k) + 1)
                    last = isinstance(k, int) and k == FT // 2 - 1
                    for kk in range(2):
                        if isinstance(k, int):
                            a = act_hi[:, 2 * k + kk, :], act_lo[:, 2 * k + kk, :]
                        else:
                            a = [m[:].rearrange("p a t -> p (a t)")[:, bass.ds((2 * k + kk) * SEQ, SEQ)]
                                 for m in (act_hi, act_lo)]
                        for n in range(KT):
                            b = slice((kk * KT + n) * P, (kk * KT + n + 1) * P)
                            first = isinstance(k, int) and k == 0 and kk == 0 and n % 2 == 0
                            ins = three(lin[:, n // 2, (n % 2) * SEQ:(n % 2 + 1) * SEQ],
                                        hi[s][:, b], lo[s][:, b], a[0], a[1],
                                        first, last and kk == 1, skip=True)
                    ins.then_inc(s_mm_done, e.adds(s_mm_done))
                e.chunks(body, head=1)

            def qkv(stage, ada=None, turn=False):
                enter(stage)
                eng.wait_ge(s_h_ready, e.past(s_h_ready))
                for k in range(6):
                    if k < 4:
                        fm(k, k, 0)
                    else:
                        tm(k)
                    if ada is not None:
                        ada_once(ada + k)
                    if turn and 1 <= k <= 4:
                        eng.wait_ge(s_turned_in, e.past(s_turned_in) + k)
                        mm(aux[:, (k - 1) % 2, :], dcon[:, DCOL["rot_p"]],
                                  work[(k - 1) % 2][:].rearrange("p a t -> p (a t)"),
                                  start=True, stop=True).then_inc(s_turned, e.adds(s_turned))

            def attention(stage, q, k, rows, flip):
                enter(stage)
                eng.wait_ge(s_qkv_made, e.past(s_qkv_made))
                for i in range(HEADS + 2):
                    if i < HEADS:
                        if i >= 2:
                            eng.wait_ge(s_maxed, e.past(s_maxed) + i - 1)
                        r = rows(i)
                        for t in range(2):
                            ins = mm(lin[:, i % 2, t * SEQ:(t + 1) * SEQ], q(i)[r, t * P:(t + 1) * P],
                                     k(i)[r, :], start=True, stop=flip is None)
                            if flip is not None:
                                if t == 0:
                                    eng.wait_ge(bias_in[i % 2], flip(i))
                                ins = mm(lin[:, i % 2, t * SEQ:(t + 1) * SEQ], bcon[:, BCOL["flip"]],
                                         bias[i % 2][:, t, :], start=False, stop=True)
                        ins.then_inc(s_scored, e.adds(s_scored))
                    h = i - 1
                    if 0 <= h < HEADS:
                        eng.wait_ge(s_normed, e.past(s_normed) + h + 1)
                        if h >= 1:
                            eng.wait_ge(s_pt_copied, e.past(s_pt_copied) + h)
                        for t in range(2):
                            for u in range(2):
                                ins = nc.tensor.transpose(lin[:, 2, u * SEQ + t * P:u * SEQ + (t + 1) * P],
                                                          work[h % 2][:, t, u * P:(u + 1) * P], ident)
                        ins.then_inc(s_transposed, e.adds(s_transposed))
                    values(i - 2, s_pt_copied)

            def values(h, ready):
                if h < 0:
                    return
                eng.wait_ge(ready, e.past(ready) + h + 1)
                if h // 2 >= 2 and h % 2 == 0:
                    eng.wait_ge(s_o_taken, e.past(s_o_taken) + h // 2 - 1)
                for u in range(2):
                    ins = mm(aux[(h % 2) * HD:(h % 2 + 1) * HD, h // 2 % 2, 0:SEQ],
                             v[:, u, h * HD:(h + 1) * HD], work[2 + h % 2][:, u, :],
                             start=(u == 0), stop=(u == 1))
                ins.then_inc(s_pv_done, e.adds(s_pv_done))

            def stick_breaking(stage):
                enter(stage)
                eng.wait_ge(s_qkv_made, e.past(s_qkv_made))
                for i in range(HEADS + 2):
                    if i < HEADS:
                        if i >= 2:
                            eng.wait_ge(s_d_made, e.past(s_d_made) + i - 1)
                        r = slice((i % 2) * HD, (i % 2 + 1) * HD)
                        for u in range(2):
                            ins = mm(lin[:, i % 2, u * SEQ:(u + 1) * SEQ],
                                     kt_[r, i // 2, u * P:(u + 1) * P], qt[r, i // 2, :],
                                     start=(u == 0), stop=(u == 1), skip_group_check=True)
                        ins.then_inc(s_scored, e.adds(s_scored))
                    h = i - 1
                    if 0 <= h < HEADS:
                        eng.wait_ge(s_sp_made, e.past(s_sp_made) + h + 1)
                        sp = work[h % 2]
                        bank = lin[:, h % 2, :]
                        mm(bank[:, 0:SEQ], dcon[:, DCOL["neg_tri"]], sp[:, 0, :], start=False, stop=False,
                           skip_group_check=True)
                        mm(bank[:, 0:SEQ], dcon[:, DCOL["neg_ones"]], sp[:, 1, :], start=False, stop=True,
                           skip_group_check=True)
                        mm(bank[:, SEQ:2 * SEQ], dcon[:, DCOL["neg_tri"]], sp[:, 1, :], start=False,
                                  stop=True, skip_group_check=True).then_inc(s_suffixed, e.adds(s_suffixed))
                    values(i - 2, s_w_made)

            def branches(stage, n, ada=None):
                enter(stage)
                for k in range(2 * n):
                    if k >= 2:
                        eng.wait_ge(s_evac, e.past(s_evac) + k - 1)
                    s = e.slot(k) % SPLIT
                    eng.wait_ge(s_lo_made, e.chunk(k) + 1)
                    for j in range(4):
                        for t in range(4):
                            b = slice((j * 4 + t) * P, (j * 4 + t + 1) * P)
                            bank = 2 * (k % 2) + j // 2
                            ins = three(lin[:, bank, (j % 2) * SEQ:(j % 2 + 1) * SEQ], hi[s][:, b],
                                        lo[s][:, b], br_hi[:, (k // 2) * 4 + t, :],
                                        br_lo[:, (k // 2) * 4 + t, :], t == 0, t == 3)
                    ins.then_inc(s_mm_done, e.adds(s_mm_done))
                    if ada is not None:
                        ada_once(ada + k)

            def out_proj(stage):
                enter(stage)
                eng.wait_ge(s_h_ready, e.past(s_h_ready))
                e.chunks(fm)

            def rows64(i):
                return slice((i % 2) * HD, (i % 2 + 1) * HD)

            eng.wait_ge(s_params_in, e.past(s_params_in) + 32)
            eng.wait_ge(s_bcon_in, 16)
            mm(aux[0:HEADS, 0, :], par[0:32, PCOL["rel_bias"]], bcon[0:32, BCOL["onehot"]],
                      start=True, stop=True).then_inc(s_rel_made, e.adds(s_rel_made))
            e.at("ada")
            eng.wait_ge(s_silu_made, e.past(s_silu_made))
            for a in range(8):
                ada_once(a)
            sums("norm1")
            qkv("dil_qkv", ada=8)
            attention("dil_attn", lambda i: qt[:, i // 2, :], lambda i: kt_[:, i // 2, :], rows64,
                      lambda i: 32 * (i // 2 + 1))
            qkv("na_qkv", ada=14)
            attention("na_attn", lambda i: qt[:, i // 2, :], lambda i: kt_[:, i // 2, :], rows64,
                      lambda i: 32 * (HEADS // 2) + 64 * (i // 2 + 1))
            enter("gates1")
            e.chunks(fm)
            branches("branch1", 2, ada=20)
            out_proj("out1")
            sums("norm2")
            enter("up1")
            eng.wait_ge(s_h_ready, e.past(s_h_ready))
            e.chunks(fm)
            down("down1")
            sums("norm3")

            with e.layers():
                e.at("ada0")
                eng.wait_ge(s_mods_made, e.past(s_mods_made))
                with e.loop(6) as i:
                    for s in range(2):
                        ada_layer(2 * i + s, s, i)
                sums("pre0")
                enter("gateup0")
                eng.wait_ge(s_h_ready, e.past(s_h_ready))

                def with_ada(k, k0, turn):
                    fm(k, k0, turn)
                    ada_layer(k + 12, k0 + 12, 2 * turn)
                e.chunks(with_ada)
                for a in (34, 35):
                    ada_layer(a, a, 0)
                down("down0")
                sums("post0")
                sums("pre1")
                qkv("moba_qkv", turn=True)
                attention("moba_attn", lambda i: qt[:, i // 2, :], lambda i: kt_[:, i // 2, :], rows64, None)
                qkv("sb_qkv")
                stick_breaking("sb_attn")

                enter("latent")
                fm(0, 0, 0)
                s = e.slot(1) % SPLIT
                eng.wait_ge(s_lo_made, e.chunk(1) + 1)
                for at, m, j in ((0, P, 0), (P, MLA_QK, 1)):
                    for t in range(KT):
                        b = slice(t * 224 + at, t * 224 + at + m)
                        ins = three(lin[0:m, 1, j * SEQ:(j + 1) * SEQ], hi[s][:, b], lo[s][:, b],
                                    h_hi[:, t, :], h_lo[:, t, :], t == 0, t == KT - 1)
                ins.then_inc(s_mm_done, e.adds(s_mm_done))
                eng.wait_ge(s_squared, e.past(s_squared) + 1)
                for j in range(2):
                    mm(norm_ps[:, 0:SEQ], ones, work[2][:, j, :], start=(j == 0), stop=(j == 1))
                eng.wait_ge(s_squared, e.past(s_squared) + 2)
                mm(norm_ps[:, SEQ:2 * SEQ], ones, work[3][:, 0, :], start=True, stop=True).then_inc(s_summed, e.adds(s_summed))
                eng.wait_ge(s_turned_in, e.past(s_turned_in) + 1)
                mm(aux[0:MLA_QK, 0, 0:SEQ], dcon[0:MLA_QK, DCOL["rot_m"]][:, 0:MLA_QK],
                          work[1][0:MLA_QK, 1, :], start=True, stop=True).then_inc(s_turned, e.adds(s_turned))

                enter("mla_up")
                eng.wait_ge(s_lat_ready, e.past(s_lat_ready))
                s = e.slot(0) % SPLIT
                eng.wait_ge(s_lo_made, e.chunk(0) + 1)
                for h in range(HEADS):
                    for t in range(2):
                        b = slice(t * 768 + h * MLA_QK, t * 768 + (h + 1) * MLA_QK)
                        ins = three(lin[0:MLA_QK, h // 2, (h % 2) * SEQ:(h % 2 + 1) * SEQ], hi[s][:, b],
                                    lo[s][:, b], lat_hi[:, t, :], lat_lo[:, t, :], t == 0, t == 1)
                ins.then_inc(s_mm_done, e.adds(s_mm_done))
                for g in range(4):
                    eng.wait_ge(s_q_turn, e.past(s_q_turn) + g + 1)
                    mm(lin[0:MLA_QK, g, :], dcon[0:MLA_QK, DCOL["rot_m"]][:, 0:MLA_QK],
                              qm[0:MLA_QK, 2 * g:2 * g + 2, :].rearrange("p a t -> p (a t)"),
                              start=True, stop=True).then_inc(s_q_turned, e.adds(s_q_turned))
                s = e.slot(1) % SPLIT
                eng.wait_ge(s_lo_made, e.chunk(1) + 1)
                for u in range(2):
                    ins = three(aux[:, u, :], lat_hi[:, 2, u * P:(u + 1) * P], lat_lo[:, 2, u * P:(u + 1) * P],
                                hi[s][:, 768:1280], lo[s][:, 768:1280], True, True)
                for h in range(HEADS):
                    if h % 2 == 0:
                        eng.wait_ge(s_evac, e.past(s_evac) + h // 2 + 1)
                    b = slice(h * MLA_QK, (h + 1) * MLA_QK)
                    ins = three(lin[0:MLA_QK, h // 2, (h % 2) * SEQ:(h % 2 + 1) * SEQ], hi[s][:, b],
                                lo[s][:, b], lat_hi[:, 2, :], lat_lo[:, 2, :], True, True)
                ins.then_inc(s_mm_done, e.adds(s_mm_done))
                attention("mla_attn", lambda i: qm[:, i, :], lambda i: km[:, i, :],
                          lambda i: slice(0, MLA_QK), None)
                enter("gates")
                e.chunks(fm)
                branches("branch", 3)
                out_proj("out")
                sums("out")
                sums("pre2")
                enter("gateup2")
                eng.wait_ge(s_h_ready, e.past(s_h_ready))
                e.chunks(fm)
                down("down2")
                sums("post2")

        @block.scalar
        def _(eng):
            e = Engine(eng, nc.scalar, S)
            act = nc.scalar.activation

            def split(c, slot, turn):
                eng.wait_ge(arrived[slot], 16 * (turn + 1))
                if not isinstance(c, int) or c >= SPLIT:
                    eng.wait_ge(s_mm_done, c - (SPLIT - 1))
                act(hi[slot % SPLIT][:], raw[:, slot, :], ACT.Copy).then_inc(s_hi_made, e.adds(s_hi_made))

            def next_split(k, k0, turn):
                split(e.chunk(k) + 1, e.slot(k0 + 1), e.round(k0 + 1, turn))

            def squares(src, ready):
                for p in range(4):
                    if ready is not None:
                        ready(p)
                    act(work[p][:], src(p), ACT.Square).then_inc(s_squared, e.adds(s_squared))

            def rsqrt(width=1.0 / D):
                eng.wait_ge(s_summed, e.past(s_summed) + 1)
                act(rs[:, 0, :], norm_ps[:, 0:SEQ], ACT.Ln, bias=eps[:, 0:1], scale=width)
                nc.scalar.drain()
                act(rs[:, 0, :], rs[:, 0, :], ACT.Exp, scale=-0.5).then_inc(s_r_made, e.adds(s_r_made))

            def pre_norm(stage):
                e.at(stage)
                eng.wait_ge(s_x_made, e.past(s_x_made))
                squares(lambda p: x[:, 2 * p:2 * p + 2, :], None)
                rsqrt()
                for p in range(4):
                    eng.wait_ge(s_flat_made, e.past(s_flat_made) + p + 1)
                    act(h_hi[:, 2 * p:2 * p + 2, :], flat[:, 2 * p:2 * p + 2, :], ACT.Copy).then_inc(s_h_hi_made, e.adds(s_h_hi_made))

            def lin_stage(stage, evac, head=0):
                e.at(stage)

                def body(k, k0, turn):
                    next_split(k, k0, turn)
                    if evac is not None:
                        evac(k, k0)
                e.chunks(body, head)

            def wait_mm(k):
                eng.wait_ge(s_mm_done, e.chunk(k) + 1)

            def o_hi(i, br):
                h = i - 3
                if h >= 0 and h % 2 == 1:
                    eng.wait_ge(s_pv_done, e.past(s_pv_done) + h + 1)
                    n = h // 2
                    act(br_hi[:, 4 * br + n, :], aux[:, n % 2, 0:SEQ], ACT.Copy).then_inc(s_o_hi_made, e.adds(s_o_hi_made))

            def load_bias(kind, i):
                b = bias[i % 2]
                for t in range(2):
                    if kind == "dil":
                        src = bass.AP(d["rel"].tensor, i * 2 * SEQ + P * (1 - t), [[1, P], [1, SEQ]])
                        eng.dma_start(b[:, t, :], src).then_inc(bias_in[i % 2], 16)
                    else:
                        for r in range(2):
                            at = i * N_RPB + (6 - 2 * t + r) * 31 - 48
                            src = bass.AP(d["rpb"].tensor, at, [[1, GRID_W], [31, ROWS], [1, GRID_W]])
                            dst = b[r * GRID_W:(r + 1) * GRID_W, t, :].rearrange("p (a c) -> p a c", a=ROWS)
                            eng.dma_start(dst, src).then_inc(bias_in[i % 2], 16)

            def attention(stage, br, kind=None):
                e.at(stage)
                for i in range(HEADS + 4):
                    if i < HEADS:
                        eng.wait_ge(s_maxed, e.past(s_maxed) + i + 1)
                        if kind is not None and i + 2 < HEADS:
                            load_bias(kind, i + 2)
                        for t in range(2):
                            ins = act(work[i % 2][:, t, :], work[i % 2][:, t, :], ACT.Exp,
                                      bias=neg_mx[:, i % 2, t:t + 1], accum_out=den[:, i % 2, t:t + 1])
                        ins.then_inc(s_exped, e.adds(s_exped))
                    h = i - 1
                    if 0 <= h < HEADS:
                        eng.wait_ge(s_transposed, e.past(s_transposed) + h + 1)
                        act(work[2 + h % 2][:], two(lin[:, 2, :]), ACT.Copy).then_inc(s_pt_copied, e.adds(s_pt_copied))
                    o_hi(i, br)

            def stick_breaking(stage, br):
                e.at(stage)
                for i in range(HEADS + 4):
                    if i < HEADS:
                        eng.wait_ge(s_scored, e.past(s_scored) + i + 1)
                        w = work[i % 2][:]
                        act(w, two(lin[:, i % 2, :]), ACT.Abs)
                        nc.scalar.drain()
                        act(w, w, ACT.Exp, scale=-1.0)
                        nc.scalar.drain()
                        act(w, w, ACT.Ln, bias=1.0).then_inc(s_logged, e.adds(s_logged))
                    h = i - 1
                    if 0 <= h < HEADS:
                        eng.wait_ge(s_d_made, e.past(s_d_made) + h + 1)
                        act(work[2 + h % 2][:], work[2 + h % 2][:], ACT.Exp).then_inc(s_w_made, e.adds(s_w_made))
                    o_hi(i, br)

            def silu_gate(k, k0):
                wait_mm(k)
                act(work[2 + k0 % 2][:, 0, :], lin[:, k0 % 2, 0:SEQ], ACT.Silu).then_inc(s_gated, e.adds(s_gated))

            def conv_mid(k, k0):
                wait_mm(k)
                for j in range(2):
                    at = PCOL["conv"].start + 4 * j
                    ins = act(work[k0 % 2][:, j, :], lin[:, k0 % 2, j * SEQ:(j + 1) * SEQ], ACT.Identity,
                              bias=par[:, bass.ds(8 * k + (at + 3), 1)], scale=par[:, bass.ds(8 * k + (at + 1), 1)])
                ins.then_inc(s_conved, e.adds(s_conved))
                eng.wait_ge(s_taps_made, e.past(s_taps_made) + k + 1)
                act(work[2 + k0 % 2][:, 0, :], work[k0 % 2][:, 1, :], ACT.Gelu_apprx_tanh).then_inc(s_gated, e.adds(s_gated))

            def sigmoid_gates(b):
                def evac(k, k0):
                    wait_mm(k)
                    for j in range(2):
                        if isinstance(k, int):
                            out = gates[:, 2 * k + j, :]
                            bb = 0.0 if b is None else lpar[:, b + 2 * k + j:b + 2 * k + j + 1]
                        else:
                            out = gates[:].rearrange("p a t -> p (a t)")[:, bass.ds((2 * k + j) * SEQ, SEQ)]
                            bb = 0.0 if b is None else lpar[:, bass.ds(2 * k + (b + j), 1)]
                        ins = act(out, lin[:, k0 % 2, j * SEQ:(j + 1) * SEQ], ACT.Sigmoid, bias=bb)
                    ins.then_inc(s_evac, e.adds(s_evac))
                return evac

            def merged_hi(last):
                def evac(k, k0):
                    if k >= last:
                        half = k - last
                        eng.wait_ge(s_merged, e.past(s_merged) + half + 1)
                        act(h_hi[:, 4 * half:4 * half + 4, :], flat[:, 4 * half:4 * half + 4, :], ACT.Copy).then_inc(s_merged_hi, e.adds(s_merged_hi))
                return evac

            def post_squares(stage):
                e.at(stage)
                squares(lambda p: flat[:, 2 * p:2 * p + 2, :], lambda p: eng.wait_ge(s_y_made, e.past(s_y_made) + p + 1))
                rsqrt()

            eng.wait_ge(s_params_in, e.past(s_params_in) + 32)
            act(cs[:, 0:16], par[:, 0:16], ACT.Silu).then_inc(s_silu_made, e.adds(s_silu_made))
            eng.wait_ge(s_rel_made, e.past(s_rel_made) + 1)
            act(rel_tab[:], aux[0:HEADS, 0, :], ACT.Copy)
            nc.scalar.drain()
            eng.dma_start(d["rel"], rel_tab[:]).then_inc(s_rel_stored, e.adds(s_rel_stored, 16))
            eng.wait_ge(s_rel_stored, e.past(s_rel_stored) + 16)
            load_bias("dil", 0)
            load_bias("dil", 1)
            split(0, 0, 0)

            e.at("norm1")
            eng.wait_ge(s_x_in, e.past(s_x_in))
            squares(lambda p: x[:, 2 * p:2 * p + 2, :], None)
            eng.wait_ge(s_eps_made, e.past(s_eps_made))
            rsqrt()
            for p in range(4):
                eng.wait_ge(s_flat_made, e.past(s_flat_made) + p + 1)
                act(h_hi[:, 2 * p:2 * p + 2, :], flat[:, 2 * p:2 * p + 2, :], ACT.Copy).then_inc(s_h_hi_made, e.adds(s_h_hi_made))
            lin_stage("dil_qkv", None)
            attention("dil_attn", 0, "dil")
            load_bias("na", 0)
            load_bias("na", 1)
            lin_stage("na_qkv", None)
            attention("na_attn", 1, "na")
            lin_stage("gates1", sigmoid_gates(None))
            lin_stage("branch1", merged_hi(2))
            lin_stage("out1", None)
            pre_norm("norm2")
            lin_stage("up1", conv_mid)
            lin_stage("down1", None, head=1)
            e.at("norm3")
            eng.wait_ge(s_x_made, e.past(s_x_made))
            squares(lambda p: x[:, 2 * p:2 * p + 2, :], None)
            rsqrt()

            with e.layers() as l:
                e.at("ada0")
                eng.wait_ge(s_x_made, e.past(s_x_made))
                eng.dma_start(lpar[:], d["lpar"][bass.ds(l, 1)].rearrange("o p n -> (o p) n")).then_inc(s_lpar_in, e.adds(s_lpar_in, 16))
                pre_norm("pre0")
                lin_stage("gateup0", silu_gate)
                lin_stage("down0", None, head=1)
                post_squares("post0")
                pre_norm("pre1")
                lin_stage("moba_qkv", None)
                attention("moba_attn", 0)
                lin_stage("sb_qkv", None)
                stick_breaking("sb_attn", 1)

                def latent(k, k0):
                    eng.wait_ge(s_y_made, e.past(s_y_made) + k + 1)
                    if k == 0:
                        act(work[2][:], work[0][:], ACT.Square).then_inc(s_squared, e.adds(s_squared))
                    else:
                        act(work[3][:, 0, :], work[1][:, 0, :], ACT.Square).then_inc(s_squared, e.adds(s_squared))
                lin_stage("latent", latent)
                eng.wait_ge(s_summed, e.past(s_summed) + 1)
                act(rs[:, 0, :], norm_ps[:, 0:SEQ], ACT.Ln, bias=eps[:, 0:1], scale=1.0 / 256)
                act(rs[:, 1, :], norm_ps[:, SEQ:2 * SEQ], ACT.Ln, bias=eps[:, 0:1], scale=1.0 / 128)
                nc.scalar.drain()
                act(rs[:], rs[:], ACT.Exp, scale=-0.5).then_inc(s_r_made, e.adds(s_r_made))
                eng.wait_ge(s_lat_made, e.past(s_lat_made) + 1)
                act(lat_hi[:, 0:2, :], work[0][:], ACT.Copy).then_inc(s_lat_hi_made, e.adds(s_lat_hi_made))
                act(lat_hi[:, 2, :], work[1][:, 0, :], ACT.Copy).then_inc(s_lat_hi_made, e.adds(s_lat_hi_made))
                lin_stage("mla_up", None)
                attention("mla_attn", 2)
                lin_stage("gates", sigmoid_gates(LCOL["b_gate"].start))
                lin_stage("branch", merged_hi(4))

                def y_squares(k, k0):
                    wait_mm(k)
                    act(work[k][:], two(lin[:, k0 % 2, :]), ACT.Square).then_inc(s_squared, e.adds(s_squared))
                lin_stage("out", y_squares)
                rsqrt()
                pre_norm("pre2")
                lin_stage("gateup2", silu_gate)
                lin_stage("down2", None, head=1)
                post_squares("post2")

        @block.vector
        def _(eng):
            e = Engine(eng, nc.vector, S)
            ve = nc.vector
            tt, ts, stt = ve.tensor_tensor, ve.tensor_scalar, ve.scalar_tensor_tensor

            def split(c, slot):
                eng.wait_ge(s_hi_made, c + 1)
                tt(lo[slot % SPLIT][:], raw[:, slot, :], hi[slot % SPLIT][:].bitcast(F32), ALU.subtract).then_inc(s_lo_made, e.adds(s_lo_made))

            def lin_stage(stage, evac, head=0):
                e.at(stage)

                def body(k, k0, turn):
                    split(e.chunk(k) + 1, e.slot(k0 + 1))
                    if evac is not None:
                        evac(k, k0)
                e.chunks(body, head)

            def wait_mm(k):
                eng.wait_ge(s_mm_done, e.chunk(k) + 1)

            def modulated(gain_, shift):
                eng.wait_ge(s_r_made, e.past(s_r_made) + 1)

                def rest(p):
                    eng.wait_ge(s_h_hi_made, e.past(s_h_hi_made) + p + 1)
                    s = slice(2 * p, 2 * p + 2)
                    tt(h_lo[:, s, :], flat[:, s, :], h_hi[:, s, :].bitcast(F32), ALU.subtract).then_inc(s_h_ready, e.adds(s_h_ready))

                for p in range(4):
                    s = slice(2 * p, 2 * p + 2)
                    tt(flat[:, s, :], x[:, s, :], over(rs[:, 0, :], 2), ALU.mult)
                    ve.drain()
                    for t in range(2 * p, 2 * p + 2):
                        ins = ts(flat[:, t, :], flat[:, t, :], gain_[:, t:t + 1], shift[:, t:t + 1], ALU.mult, ALU.add)
                    ins.then_inc(s_flat_made, e.adds(s_flat_made))
                    if p:
                        rest(p - 1)
                rest(3)

            def residual(s):
                eng.wait_ge(s_r_made, e.past(s_r_made) + 1)
                for p in range(4):
                    a = slice(2 * p, 2 * p + 2)
                    tt(flat[:, a, :], flat[:, a, :], over(rs[:, 0, :], 2), ALU.mult)
                    ve.drain()
                    for t in range(2 * p, 2 * p + 2):
                        ins = stt(x[:, t, :], flat[:, t, :], post_gain[:, 8 * s + t:8 * s + t + 1], x[:, t, :],
                                  ALU.mult, ALU.add)
                    ins.then_inc(s_x_made, e.adds(s_x_made))

            def post(stage, s):
                e.at(stage)
                eng.wait_ge(s_mm_done, e.chunk(0))
                for p in range(4):
                    ve.tensor_copy(flat[:, 2 * p:2 * p + 2, :], two(lin[:, p, :])).then_inc(s_y_made, e.adds(s_y_made))
                ve.drain().then_inc(s_evac_y, e.adds(s_evac_y))
                residual(s)

            def modulations(stage, s):
                a = 24 * s
                tt(mod[:, a:a + 24], ada_ps[:, a:a + 24], lpar[:, a:a + 24], ALU.add)
                ve.drain()
                pre, post_ = LCOL["norm_pre"].start + 8 * s, LCOL["norm_post"].start + 8 * s
                stt(gain[:, 8 * s:8 * s + 8], mod[:, a + 8:a + 16], 1.0, lpar[:, pre:pre + 8], ALU.add, ALU.mult)
                stt(post_gain[:, 8 * s:8 * s + 8], mod[:, a + 16:a + 24], 1.0, lpar[:, post_:post_ + 8],
                    ALU.add, ALU.mult)
                ve.drain()
                ts(post_gain[:, 8 * s:8 * s + 8], post_gain[:, 8 * s:8 * s + 8], 1.0 if s == 1 else 0.5,
                          None, ALU.mult).then_inc(s_mods_made, e.adds(s_mods_made))
                ve.drain()

            def qkv(stage, turn=False):
                def evac(k, k0):
                    wait_mm(k)
                    bank = two(lin[:, k % 2, :])
                    scale = HD ** -0.5 if k < 2 else 1.0
                    dst = [qt, qt, kt_, kt_][k][:, 2 * (k % 2):2 * (k % 2) + 2, :] if k < 4 else None
                    if k < 4 and not turn:
                        ts(dst, bank, scale, None, ALU.mult).then_inc(s_evac, e.adds(s_evac))
                    elif k < 4:
                        ins = ts(work[k % 2][:], bank, scale, None, ALU.mult).then_inc(s_evac, e.adds(s_evac))
                        ve.drain()
                        ve.tensor_copy(dst, work[k % 2][:]).then_inc(s_turned_in, e.adds(s_turned_in))
                    else:
                        dst = v[:, :, (k - 4) * SEQ:(k - 3) * SEQ]
                        ve.tensor_copy(dst, bank).then_inc(s_evac, e.adds(s_evac))
                    if turn and 1 <= k <= 4:
                        j = k - 1
                        dst = [qt, qt, kt_, kt_][j][:, 2 * (j % 2):2 * (j % 2) + 2, :]
                        eng.wait_ge(s_turned, e.past(s_turned) + j + 1)
                        tt(work[2][:], two(aux[:, j % 2, :]), over(dcon[:, DCOL["sin_p"]], 2), ALU.mult)
                        tt(dst, dst, over(dcon[:, DCOL["cos_p"]], 2), ALU.mult)
                        ve.drain()
                        tt(dst, dst, work[2][:], ALU.add)
                        ve.drain()
                lin_stage(stage, evac)
                ve.drain().then_inc(s_qkv_made, e.adds(s_qkv_made))

            def o_lo(i, br):
                h = i - 3
                if h >= 0 and h % 2 == 1:
                    n = h // 2
                    eng.wait_ge(s_o_hi_made, e.past(s_o_hi_made) + n + 1)
                    tt(br_lo[:, 4 * br + n, :], aux[:, n % 2, 0:SEQ],
                              br_hi[:, 4 * br + n, :].bitcast(F32), ALU.subtract).then_inc(s_o_taken, e.adds(s_o_taken))

            def attention(stage, br, mask):
                e.at(stage)
                for i in range(HEADS + 4):
                    if i < HEADS:
                        eng.wait_ge(s_scored, e.past(s_scored) + i + 1)
                        if e.in_layers():
                            eng.sem_inc(s_passed, 1)
                        for t in range(2):
                            ve.tensor_tensor_reduce(out=work[i % 2][:, t, :], in0=lin[:, i % 2, t * SEQ:(t + 1) * SEQ],
                                                    in1=mask[:, t * SEQ:(t + 1) * SEQ], scale=1.0, scalar=-3e38,
                                                    op0=ALU.add, op1=ALU.max, accum_out=mx[:, i % 2, t:t + 1])
                        ve.drain()
                        ts(neg_mx[:, i % 2, :], mx[:, i % 2, :], -1.0, None, ALU.mult).then_inc(s_maxed, e.adds(s_maxed))
                    h = i - 1
                    if 0 <= h < HEADS:
                        eng.wait_ge(s_exped, e.past(s_exped) + h + 1)
                        ve.reciprocal(rden[:, h % 2, :], den[:, h % 2, :])
                        ve.drain()
                        for t in range(2):
                            ins = ts(work[h % 2][:, t, :], work[h % 2][:, t, :], rden[:, h % 2, t:t + 1], None,
                                     ALU.mult)
                        ins.then_inc(s_normed, e.adds(s_normed))
                    o_lo(i, br)

            def stick_breaking(stage, br):
                e.at(stage)
                for i in range(HEADS + 4):
                    if i < HEADS:
                        eng.wait_ge(s_logged, e.past(s_logged) + i + 1)
                        w = work[i % 2][:]
                        stt(w, two(lin[:, i % 2, :]), 0.0, w, ALU.max, ALU.add)
                        ve.drain()
                        tt(w, w, two(dcon[:, DCOL["sb_mul"]]), ALU.mult).then_inc(s_sp_made, e.adds(s_sp_made))
                    h = i - 1
                    if 0 <= h < HEADS:
                        eng.wait_ge(s_suffixed, e.past(s_suffixed) + h + 1)
                        tt(work[2 + h % 2][:], two(lin[:, h % 2, :]), two(dcon[:, DCOL["sb_add"]]), ALU.add).then_inc(s_d_made, e.adds(s_d_made))
                    o_lo(i, br)

            def split_act(k, a):
                sides = [m[:].rearrange("p a t -> p (a t)")[:, bass.ds(k * SEQ, SEQ)] if not isinstance(k, int)
                         else m[:, k, :] for m in (act_hi, act_lo)]
                ve.tensor_copy(sides[0], a)
                ve.drain()
                return tt(sides[1], a, sides[0].bitcast(F32), ALU.subtract)

            def swiglu(k, k0):
                eng.wait_ge(s_gated, e.past(s_gated) + k + 1)
                w = work[2 + k0 % 2]
                tt(w[:, 1, :], w[:, 0, :], lin[:, k0 % 2, SEQ:2 * SEQ], ALU.mult).then_inc(s_evac, e.adds(s_evac))
                ve.drain()
                split_act(k, w[:, 1, :]).then_inc(s_act_made, e.adds(s_act_made))

            def conv_glu(k, k0):
                eng.wait_ge(s_conved, e.past(s_conved) + k + 1)
                for j in (1, 0):
                    at = PCOL["conv"].start + 4 * j
                    u = work[k0 % 2][:, j, :]
                    p = lin[:, k0 % 2, j * SEQ:(j + 1) * SEQ]
                    stt(u[:, 1:SEQ], p[:, 0:SEQ - 1], par[:, bass.ds(8 * k + at, 1)], u[:, 1:SEQ], ALU.mult, ALU.add)
                    ve.drain()
                    ins = stt(u[:, 0:SEQ - 1], p[:, 1:SEQ], par[:, bass.ds(8 * k + (at + 2), 1)], u[:, 0:SEQ - 1],
                              ALU.mult, ALU.add)
                    ins.then_inc((s_taps_made if j == 1 else s_evac), e.adds((s_taps_made if j == 1 else s_evac)))
                ve.drain()
                eng.wait_ge(s_gated, e.past(s_gated) + k + 1)
                w = work[2 + k0 % 2]
                tt(w[:, 1, :], w[:, 0, :], work[k0 % 2][:, 0, :], ALU.mult)
                ve.drain()
                split_act(k, w[:, 1, :]).then_inc(s_act_made, e.adds(s_act_made))

            def merge(last):
                def evac(k, k0):
                    wait_mm(k)
                    n, half = k // 2, k % 2
                    a = slice(4 * half, 4 * half + 4)
                    g = gates[:, 8 * n + 4 * half:8 * n + 4 * half + 4, :]
                    y = lin[:, 2 * half:2 * half + 2, :].rearrange("p b (a t) -> p (b a) t", a=2)
                    if n == 0:
                        tt(flat[:, a, :], g, y, ALU.mult).then_inc(s_evac, e.adds(s_evac))
                    else:
                        tt(g, g, y, ALU.mult).then_inc(s_evac, e.adds(s_evac))
                        ve.drain()
                        ins = tt(flat[:, a, :], flat[:, a, :], g, ALU.add)
                        if k >= last:
                            ins.then_inc(s_merged, e.adds(s_merged))
                            eng.wait_ge(s_merged_hi, e.past(s_merged_hi) + half + 1)
                            tt(h_lo[:, a, :], flat[:, a, :], h_hi[:, a, :].bitcast(F32), ALU.subtract).then_inc(s_h_ready, e.adds(s_h_ready, 2))
                return evac

            eng.wait_ge(s_params_in, e.past(s_params_in) + 32)
            split(0, 0)
            e.at("ada")
            eng.wait_ge(s_ada_used, e.past(s_ada_used) + 8)
            tt(mod[:, 0:16], ada_ps[:, 0:16], par[:, PCOL["b_ada"]][:, 0:16], ALU.add)
            ve.drain()
            stt(gain[:, 0:8], mod[:, 8:16], 1.0, par[:, PCOL["g_mix"]], ALU.add, ALU.mult)
            ve.drain()
            e.at("norm1")
            modulated(gain, mod)
            qkv("dil_qkv")
            eng.wait_ge(s_bcon_in, e.past(s_bcon_in))
            attention("dil_attn", 0, bcon[:, BCOL["dil"]])
            qkv("na_qkv")
            attention("na_attn", 1, bcon[:, BCOL["na"]])
            lin_stage("gates1", None)
            lin_stage("branch1", merge(2))
            e.at("mods1")
            eng.wait_ge(s_ada_used, e.past(s_ada_used))
            tt(mod[:, 16:48], ada_ps[:, 16:48], par[:, PCOL["b_ada"]][:, 16:48], ALU.add)
            ve.drain()
            stt(gain[:, 8:16], mod[:, 32:40], 1.0, par[:, PCOL["g_ffn"]], ALU.add, ALU.mult)
            ve.drain().then_inc(s_mods_made, e.adds(s_mods_made))

            def out_residual(k, k0):
                wait_mm(k)
                for j in range(2):
                    t = 2 * k + j
                    ins = stt(x[:, t, :], lin[:, k0 % 2, j * SEQ:(j + 1) * SEQ], mod[:, 16 + t:17 + t], x[:, t, :],
                              ALU.mult, ALU.add)
                ins.then_inc(s_evac, e.adds(s_evac))
                if k == 3:
                    ve.drain().then_inc(s_x_made, e.adds(s_x_made))
            lin_stage("out1", out_residual)
            e.at("norm2")
            modulated(gain[:, 8:16], mod[:, 24:32])
            lin_stage("up1", conv_glu)
            lin_stage("down1", None, head=1)
            eng.wait_ge(s_mm_done, e.chunk(FT // 2))
            for t in range(KT):
                ins = stt(x[:, t, :], lin[:, t // 2, (t % 2) * SEQ:(t % 2 + 1) * SEQ], mod[:, 40 + t:41 + t],
                          x[:, t, :], ALU.mult, ALU.add)
            ins.then_inc(s_evac, e.adds(s_evac))
            ve.drain().then_inc(s_x_made, e.adds(s_x_made))
            e.at("norm3")
            eng.wait_ge(s_r_made, e.past(s_r_made) + 1)
            tt(flat[:], x[:], over(rs[:, 0, :], KT), ALU.mult)
            ve.drain()
            g = PCOL["g_final"].start
            for t in range(KT):
                ins = ts(x[:, t, :], flat[:, t, :], par[:, g + t:g + t + 1], None, ALU.mult)
            ins.then_inc(s_x_made, e.adds(s_x_made))

            with e.layers():
                e.at("ada0")
                eng.wait_ge(s_lpar_in, e.past(s_lpar_in) + 16)
                eng.wait_ge(s_ada_used, e.past(s_ada_used) + 12)
                modulations("ada0", 0)
                e.at("pre0")
                modulated(gain[:, 0:8], mod[:, 0:8])
                lin_stage("gateup0", swiglu)
                eng.wait_ge(s_ada_used, e.past(s_ada_used) + 24)
                modulations("gateup0", 1)
                modulations("gateup0", 2)
                lin_stage("down0", None, head=1)
                post("post0", 0)
                e.at("pre1")
                modulated(gain[:, 8:16], mod[:, 24:32])
                eng.wait_ge(s_dcon_in, e.past(s_dcon_in))
                qkv("moba_qkv", turn=True)
                attention("moba_attn", 0, con[:, CCOL["causal"]])
                qkv("sb_qkv")
                stick_breaking("sb_attn", 1)

                def latent(k, k0):
                    wait_mm(k)
                    if k == 0:
                        ve.tensor_copy(work[0][:], two(lin[:, 0, :])).then_inc(s_y_made, e.adds(s_y_made))
                    else:
                        ve.tensor_copy(work[1][:, 0, :], lin[:, 1, 0:SEQ]).then_inc(s_y_made, e.adds(s_y_made))
                        ve.tensor_copy(work[1][0:MLA_QK, 1, :], lin[0:MLA_QK, 1, SEQ:2 * SEQ]).then_inc(s_turned_in, e.adds(s_turned_in))
                lin_stage("latent", latent)
                eng.wait_ge(s_turned, e.past(s_turned) + 1)
                kr = work[1][0:MLA_QK, 1, :]
                rot = work[3][0:MLA_QK, 1, :]
                tt(rot, aux[0:MLA_QK, 0, 0:SEQ], dcon[0:MLA_QK, DCOL["sin_m"]], ALU.mult)
                tt(kr, kr, dcon[0:MLA_QK, DCOL["cos_m"]], ALU.mult)
                ve.drain()
                tt(kr, kr, rot, ALU.add)
                eng.wait_ge(s_r_made, e.past(s_r_made) + 1)
                tt(work[0][:], work[0][:], over(rs[:, 0, :], 2), ALU.mult)
                tt(work[1][:, 0, :], work[1][:, 0, :], rs[:, 1, :], ALU.mult)
                ve.drain()
                for t in range(2):
                    q = LCOL["q_norm"].start + t
                    ts(work[0][:, t, :], work[0][:, t, :], lpar[:, q:q + 1], None, ALU.mult)
                q = LCOL["kv_norm"].start
                ts(work[1][:, 0, :], work[1][:, 0, :], lpar[:, q:q + 1], None, ALU.mult).then_inc(s_lat_made, e.adds(s_lat_made))
                eng.wait_ge(s_squared, e.past(s_squared) + 2)
                eng.wait_ge(s_lat_hi_made, e.past(s_lat_hi_made) + 2)
                tt(lat_lo[:, 0:2, :], work[0][:], lat_hi[:, 0:2, :].bitcast(F32), ALU.subtract)
                tt(lat_lo[:, 2, :], work[1][:, 0, :], lat_hi[:, 2, :].bitcast(F32), ALU.subtract).then_inc(s_lat_ready, e.adds(s_lat_ready))
                ve.drain().then_inc(s_evac, e.adds(s_evac))

                def mla_up(k, k0):
                    wait_mm(k)
                    if k == 0:
                        for g in range(4):
                            ts(qm[0:MLA_QK, 2 * g:2 * g + 2, :], two(lin[0:MLA_QK, g, :]), MLA_QK ** -0.5, None,
                                      ALU.mult).then_inc(s_q_turn, e.adds(s_q_turn))
                        for g in range(4):
                            eng.wait_ge(s_q_turned, e.past(s_q_turned) + g + 1)
                            q = qm[0:MLA_QK, 2 * g:2 * g + 2, :]
                            rot = work[2 + g % 2][0:MLA_QK, :, :]
                            tt(rot, two(lin[0:MLA_QK, g, :]), over(dcon[0:MLA_QK, DCOL["sin_m"]], 2), ALU.mult).then_inc(s_evac, e.adds(s_evac))
                            tt(q, q, over(dcon[0:MLA_QK, DCOL["cos_m"]], 2), ALU.mult)
                            ve.drain()
                            tt(q, q, rot, ALU.add)
                    else:
                        for g in range(4):
                            tt(km[0:MLA_QK, 2 * g:2 * g + 2, :], two(lin[0:MLA_QK, g, :]), over(kr, 2), ALU.add)
                        for u in range(2):
                            ins = ve.tensor_copy(v[:, u, :], aux[:, u, :])
                        ins.then_inc(s_evac, e.adds(s_evac))
                        ve.drain().then_inc(s_qkv_made, e.adds(s_qkv_made))
                lin_stage("mla_up", mla_up)
                attention("mla_attn", 2, con[:, CCOL["causal"]])
                lin_stage("gates", None)
                lin_stage("branch", merge(4))

                def take_y(k, k0):
                    wait_mm(k)
                    eng.wait_ge(s_squared, e.past(s_squared) + k + 1)
                    ve.tensor_copy(flat[:, 2 * k:2 * k + 2, :], two(lin[:, k0 % 2, :])).then_inc(s_evac, e.adds(s_evac))
                lin_stage("out", take_y)
                residual(1)
                e.at("pre2")
                modulated(gain[:, 16:24], mod[:, 48:56])
                lin_stage("gateup2", swiglu)
                lin_stage("down2", None, head=1)
                post("post2", 2)
    return S.seen


def constants():
    f = np.float32
    t = np.arange(SEQ)
    con = np.zeros((P, NCCOL), f)
    con[:, CCOL["ident"]] = np.eye(P)
    con[:, CCOL["ones"]] = 1.0

    def by_query(allowed_log):
        return allowed_log.reshape(2, P, SEQ).transpose(1, 0, 2).reshape(P, 2 * SEQ)

    q, k = t[:, None], t[None, :]
    con[:, CCOL["causal"]] = by_query(np.where(k <= q, 0.0, MASKED))

    b = np.zeros((P, NBCOL), f)
    b[:, BCOL["flip"]] = np.eye(P)[::-1]
    delta = k - q
    count = (np.abs(delta) <= 64) * 1 + (delta % 4 == 0) * 1 + (delta % 16 == 0) * 1
    b[:, BCOL["dil"]] = by_query(np.where(count > 0, np.log(np.maximum(count, 1)), MASKED))
    cq, ck = q % GRID_W, k % GRID_W
    start = np.clip(cq - 8, 0, GRID_W - 16)
    b[:, BCOL["na"]] = by_query(np.where((ck >= start) & (ck < start + 16), 0.0, MASKED))
    rel = np.arange(-(SEQ - 1), SEQ + 1)
    a = np.abs(rel)
    large = 8 + (np.log(np.maximum(a, 1).astype(f) / 8) / f(np.log(1024 / 8)) * 8).astype(np.int32)
    bucket = np.where(rel > 0, 16, 0) + np.where(a < 8, a, np.minimum(large, 15))
    b[0:32, BCOL["onehot"]] = bucket[None, :] == np.arange(32)[:, None]

    c = np.zeros((P, NDCOL), f)
    j, i = np.arange(P)[:, None], np.arange(P)[None, :]
    c[:, DCOL["neg_tri"]] = np.where(j >= i, -1.0, 0.0)
    c[:, DCOL["neg_ones"]] = -1.0

    def rotary(n_rot, at, width, rot, cos, sin):
        inv = (f(500000.0) ** (-np.arange(0, n_rot, 2, dtype=f) / n_rot)).astype(f)
        ang = t.astype(f)[:, None] * inv[None, :]
        half = n_rot // 2
        m = np.zeros((P, P), f)
        cc, ss = np.ones((P, SEQ), f), np.zeros((P, SEQ), f)
        for base in range(0, P - width + 1, width):
            for r in range(n_rot):
                row, partner = base + at + r, base + at + (r + half) % n_rot
                m[partner, row] = -1.0 if r < half else 1.0
                cc[row], ss[row] = np.cos(ang[:, r % half]), np.sin(ang[:, r % half])
        c[:, DCOL[rot]], c[:, DCOL[cos]], c[:, DCOL[sin]] = m, cc, ss

    rotary(16, 0, HD, "rot_p", "cos_p", "sin_p")
    rotary(MLA_ROPE, MLA_NOPE, MLA_QK, "rot_m", "cos_m", "sin_m")
    both = lambda m: m.T.reshape(2, P, SEQ).transpose(1, 0, 2).reshape(P, 2 * SEQ)
    c[:, DCOL["sb_add"]] = both(np.where(k < q, 0.0, MASKED))
    c[:, DCOL["sb_mul"]] = both(np.where(k < q, 1.0, 0.0))
    return con, b, c


def tiles(w):
    kk, n = w.shape
    return w.reshape(kk // P, P, n // P, P).transpose(2, 1, 0, 3)


def fm_chunks(w, order=None):
    t = tiles(w)
    if order is not None:
        t = t[order]
    n = t.shape[0] // 2
    return t.reshape(n, 2, P, KT, P).transpose(0, 2, 1, 3, 4).reshape(n, P, CH)


def tm_chunks(w):
    n = w.shape[1] // SEQ
    return w.reshape(KT, P, n, SEQ).transpose(2, 1, 0, 3).reshape(n, P, CH)


def down_chunks(w):
    n = w.shape[0] // (2 * P)
    return w.reshape(n, 2, P, KT, P).transpose(0, 2, 1, 3, 4).reshape(n, P, CH)


def branch_chunks(w):
    t = tiles(w)
    return t.reshape(2, 4, P, 4, P).transpose(0, 2, 1, 3, 4).reshape(2, P, CH)


def padded(w):
    out = np.zeros((1, P, CH), np.float32)
    out[0, :, :w.shape[1]] = w
    return out


def qkv_chunks(w):
    return [fm_chunks(w[:, :1024]), tm_chunks(w[:, 1024:])]


def vector(a):
    return a.reshape(-1, P).T


def pairs(n):
    return np.stack([np.arange(n), n + np.arange(n)], 1).reshape(-1)


def layouts(i):
    w = []
    win = i["w_in"][0]
    w += qkv_chunks(win[:, 0:1536]) + qkv_chunks(win[:, 1536:3072]) + [fm_chunks(win[:, 3072:])]
    w += [branch_chunks(i["w_branch_dil"][0]), branch_chunks(i["w_branch_na"][0]), fm_chunks(i["w_out"][0])]
    w += [fm_chunks(i["w_up"][0], pairs(FT)), down_chunks(i["w_down"][0])]
    for l in range(LAYERS):
        def ffn(s):
            g, u = i["ffn_w_gate_2"][l, s], i["ffn_w_up_2"][l, s]
            return [fm_chunks(np.concatenate([g, u], 1), pairs(FT)), down_chunks(i["ffn_w_down_2"][l, s])]
        win = i["mix_w_in_2"][l]
        w += ffn(0) + qkv_chunks(win[:, 0:1536]) + qkv_chunks(win[:, 1536:3072]) + [fm_chunks(win[:, 3072:3328])]
        lat = np.zeros((KT, P, 224), np.float32)
        lat[:, :, 0:128] = win[:, 3328:3456].reshape(KT, P, 128)
        lat[:, :, 192:224] = win[:, 3456:3488].reshape(KT, P, 32)
        w.append(padded(lat.transpose(1, 0, 2).reshape(P, -1)))
        w.append(padded(i["mla_w_uq_2"][l].reshape(2, P, 768).transpose(1, 0, 2).reshape(P, -1)))
        kv = i["mla_w_ukv_2"][l].reshape(P, HEADS, 128)
        up = np.zeros((P, HEADS, MLA_QK), np.float32)
        up[:, :, 0:64] = kv[:, :, 0:64]
        w.append(padded(np.concatenate([up.reshape(P, -1), kv[:, :, 64:].reshape(P, -1)], 1)))
        w.append(fm_chunks(win[:, 3488:]))
        w += [branch_chunks(i["mix_w_branch_2"][l, n]) for n in range(3)] + [fm_chunks(i["mix_w_out_2"][l])]
        w += ffn(1)
    w.append(np.zeros((1, P, CH), np.float32))
    ada = np.concatenate([fm_chunks(i["w_ada"][0])] + [fm_chunks(i["ada_w_2"][l]) for l in range(LAYERS)])

    par = np.zeros((P, NPCOL), np.float32)
    for name in ("c", "c_2", "b_ada", "g_mix", "g_ffn", "g_final"):
        par[:, PCOL[name]] = vector(i[name].reshape(-1))
    taps = np.concatenate([i["conv_w"][0], i["conv_b"]], 0)
    par[:, PCOL["conv"]] = taps.reshape(4, 2, FT, P).transpose(3, 2, 1, 0).reshape(P, -1)
    par[0:32, PCOL["rel_bias"]] = i["rel_bias"]
    lpar = np.zeros((LAYERS, P, NLCOL), np.float32)
    for l in range(LAYERS):
        for name, key in (("ada_b", "ada_b_2"), ("norm_pre", "norm_pre_2"), ("norm_post", "norm_post_2"),
                          ("b_gate", "mix_b_gate_2"), ("q_norm", "mla_q_norm_2"), ("kv_norm", "mla_kv_norm_2")):
            lpar[l][:, LCOL[name]] = vector(i[key][l].reshape(-1))
    con, bcon, dcon = constants()
    return {"w": np.concatenate(w), "ada": ada, "par": par, "lpar": lpar, "con": con, "bcon": bcon, "dcon": dcon,
            "x": np.ascontiguousarray(i["x"][0].T.reshape(KT, P, SEQ).transpose(1, 0, 2)),
            "rpb": np.ascontiguousarray(i["na_rpb"][0].reshape(HEADS, N_RPB))}


def tensors(nc, arrays):
    d = {n: nc.dram_tensor(f"in_{n}", a.shape, F32, kind="ExternalInput").ap() for n, a in arrays.items()}
    d["rel"] = nc.dram_tensor("rel_rows", [HEADS, 2 * SEQ], F32, kind="Internal").ap()
    d["out"] = nc.dram_tensor("out_x", [P, KT, SEQ], F32, kind="ExternalOutput").ap()
    return d


def kernel(**inputs):
    import concourse.bacc as bacc
    from concourse.bass_utils import run_bass_kernel_spmd

    arrays = layouts({n: np.asarray(a) for n, a in inputs.items()})
    draft = bacc.Bacc("TRN2", target_bir_lowering=False, num_devices=1)
    totals = program(draft, tensors(draft, arrays), {})
    nc = bacc.Bacc("TRN2", target_bir_lowering=False, num_devices=1)
    program(nc, tensors(nc, arrays), totals)
    r = run_bass_kernel_spmd(nc, [{f"in_{n}": a for n, a in arrays.items()}], core_ids=[0])
    out = r.results[0]["out_x"]
    return np.ascontiguousarray(out.transpose(2, 1, 0).reshape(1, SEQ, D))
```

```python
from contextlib import ExitStack, contextmanager

import numpy as np

import concourse.bass as bass
from concourse import mybir

F32 = mybir.dt.float32
F32R = mybir.dt.float32r
ACT = mybir.ActivationFunctionType
ALU = mybir.AluOpType

P = 128
SEQ = 256
D = 1024
KT = D // P
HEADS = 8
HD = 64
D_FF = 2816
FT = D_FF // P
GRID_W = 64
ROWS = SEQ // GRID_W
LAYERS = 2
MLA_QK = 96
MLA_NOPE = 64
MLA_ROPE = 32
EPS = 1e-6
MASKED = -1e30
CH = 16 * P
RAW = 4
SPLIT = 2
N_RPB = 15 * 31

ONCE = [("start", 0), ("ada", 0), ("norm1", 0), ("dil_qkv", 6), ("dil_attn", 0), ("na_qkv", 6),
        ("na_attn", 0), ("gates1", 8), ("branch1", 4), ("mods1", 0), ("out1", 4), ("norm2", 0),
        ("up1", FT), ("down1", FT // 2), ("norm3", 0)]
LAYER = [("ada0", 0), ("pre0", 0), ("gateup0", FT), ("down0", FT // 2), ("post0", 0),
         ("pre1", 0), ("moba_qkv", 6), ("moba_attn", 0), ("sb_qkv", 6), ("sb_attn", 0),
         ("latent", 2), ("mla_up", 2), ("mla_attn", 0), ("gates", 12), ("branch", 6), ("out", 4),
         ("pre2", 0), ("gateup2", FT), ("down2", FT // 2), ("post2", 0)]
STAGES = ONCE + LAYER + [("end", 0)]
FIRST_CHUNK = {}
_at = 0
for _name, _n in STAGES:
    FIRST_CHUNK[_name] = _at
    _at += _n
ONCE_CHUNKS = sum(n for _, n in ONCE)
LAYER_CHUNKS = sum(n for _, n in LAYER)
assert LAYER_CHUNKS % RAW == 0
CHUNKS = ONCE_CHUNKS + LAYERS * LAYER_CHUNKS
ADA_ONCE = 24
ADA_LAYER = 36
ADA_CHUNKS = ADA_ONCE + LAYERS * ADA_LAYER

def columns(*parts):
    at, out = 0, {}
    for name, n in parts:
        out[name] = slice(at, at + n)
        at += n
    return out, at


PCOL, NPCOL = columns(("c", 8), ("c_2", 8), ("b_ada", 48), ("g_mix", 8), ("g_ffn", 8), ("g_final", 8),
                      ("conv", 8 * FT), ("rel_bias", 8))
LCOL, NLCOL = columns(("ada_b", 72), ("norm_pre", 24), ("norm_post", 24), ("b_gate", 24),
                      ("q_norm", 2), ("kv_norm", 1))
CCOL, NCCOL = columns(("ident", P), ("ones", P), ("causal", 2 * SEQ))
BCOL, NBCOL = columns(("flip", P), ("dil", 2 * SEQ), ("na", 2 * SEQ), ("onehot", 2 * SEQ))
DCOL, NDCOL = columns(("neg_tri", P), ("neg_ones", P), ("rot_p", P), ("rot_m", P), ("cos_p", SEQ),
                      ("sin_p", SEQ), ("cos_m", SEQ), ("sin_m", SEQ), ("sb_add", 2 * SEQ),
                      ("sb_mul", 2 * SEQ))


class Signals:

    def __init__(self, nc, ctx, totals):
        self.nc, self.ctx = nc, ctx
        self.names = {}
        self.totals = totals
        self.seen = {}

    def make(self, name):
        sem = self.ctx.enter_context(self.nc.semaphore(name))
        self.names[id(sem)] = name
        return sem

    def base(self, name, stage, l):
        total = 0
        for s, _ in ONCE:
            if s == stage:
                return total
            total += self.totals.get((s, name), 0)
        round_ = sum(self.totals.get((s, name), 0) for s, _ in LAYER)
        for s, _ in LAYER:
            if s == stage:
                return total + l * round_
            total += self.totals.get((s, name), 0)
        return total + (LAYERS - 1) * round_


class Engine:

    def __init__(self, eng, ops, signals):
        self.eng, self.ops, self.s = eng, ops, signals
        self.stage, self.l, self.times = "start", 0, 1

    def at(self, stage):
        self.stage = stage

    def past(self, sem):
        return self.s.base(self.s.names[id(sem)], self.stage, self.l)

    def adds(self, sem, n=1):
        key = self.stage, self.s.names[id(sem)]
        self.s.seen[key] = self.s.seen.get(key, 0) + n * self.times
        return n

    def in_layers(self):
        return not isinstance(self.l, int)

    @contextmanager
    def loop(self, n):
        self.times *= n
        if self.in_layers():
            self.eng.sem_inc(self.s.passed, 1)
        with self.eng.Fori(0, n) as i:
            yield i
        self.times //= n

    @contextmanager
    def layers(self):
        with self.eng.Fori(0, LAYERS) as l:
            self.l = l
            yield l
        self.l = LAYERS - 1

    def chunk(self, k):
        c = FIRST_CHUNK[self.stage] + k
        return c if self.stage in dict(ONCE) else self.l * LAYER_CHUNKS + c

    def round(self, k0, turn):
        c = (FIRST_CHUNK[self.stage] + k0) // RAW + turn
        return c if self.stage in dict(ONCE) else self.l * (LAYER_CHUNKS // RAW) + c

    def chunks(self, body, head=0):
        n = dict(STAGES)[self.stage]
        for k in range(head):
            body(k, k, 0)
        turns = (n - head) // RAW
        k = head
        if turns > 1:
            with self.loop(turns) as i:
                for j in range(RAW):
                    body(RAW * i + (head + j), head + j, i)
            k = head + RAW * turns
        while k < n:
            body(k, k, 0)
            k += 1

    def slot(self, k0):
        return (FIRST_CHUNK[self.stage] + k0) % RAW


def program(nc, d, totals):
    with ExitStack() as ctx:
        def sb(name, shape, dt=F32, scope=ctx):
            return scope.enter_context(nc.sbuf_tensor(name, shape, dt))

        raw = sb("raw", [P, RAW, CH])
        hi = [sb(f"hi{i}", [P, CH], F32R) for i in range(SPLIT)]
        lo = [sb(f"lo{i}", [P, CH], F32R) for i in range(SPLIT)]
        ada_w = [sb(f"ada_w{i}", [P, CH]) for i in range(2)]
        x = sb("x", [P, KT, SEQ])
        h_hi = sb("h_hi", [P, KT, SEQ], F32R)
        h_lo = sb("h_lo", [P, KT, SEQ], F32R)
        work = [sb(f"work{i}", [P, 2, SEQ]) for i in range(4)]
        rs = sb("rs", [P, 2, SEQ])
        par = sb("par", [P, NPCOL])
        lpar = sb("lpar", [P, NLCOL])
        con = sb("con", [P, NCCOL])
        cs = sb("cs", [P, 16])
        mod = sb("mod", [P, 72])
        gain = sb("gain", [P, 24])
        post_gain = sb("post_gain", [P, 24])
        eps = sb("eps", [P, 1])
        mx = sb("mx", [P, 2, 2])
        neg_mx = sb("neg_mx", [P, 2, 2])
        den = sb("den", [P, 2, 2])
        rden = sb("rden", [P, 2, 2])

        with ExitStack() as scope:
            act_hi = sb("act_hi", [P, FT, SEQ], F32R, scope)
            act_lo = sb("act_lo", [P, FT, SEQ], F32R, scope)
        with ExitStack() as scope:
            flat = sb("flat", [P, KT, SEQ], F32, scope)
        with ExitStack() as scope:
            qm = sb("qm", [P, HEADS, SEQ], F32, scope)
            km = sb("km", [P, HEADS, SEQ], F32, scope)
            v = sb("v", [P, 2, 512], F32, scope)
            br_hi = sb("br_hi", [P, 12, SEQ], F32R, scope)
            br_lo = sb("br_lo", [P, 12, SEQ], F32R, scope)
            gates = sb("gates", [P, 24, SEQ], F32, scope)
            lat_hi = sb("lat_hi", [P, 3, SEQ], F32R, scope)
            lat_lo = sb("lat_lo", [P, 3, SEQ], F32R, scope)
            dcon = sb("dcon", [P, NDCOL], F32, scope)
        with ExitStack() as scope:
            sb("below", [P, (2 * HEADS + 4 + 2 * 12 + 16) * SEQ], F32, scope)
            bcon = sb("bcon", [P, NBCOL], F32, scope)
            rel_tab = sb("rel_tab", [HEADS, 2 * SEQ], F32, scope)
            bias = [sb(f"bias{i}", [P, 2, SEQ], F32, scope) for i in range(2)]
        qt = qm[:, 0:4, :]
        kt_ = km[:, 0:4, :]

        lin = ctx.enter_context(nc.psum_tensor("lin", [P, 4, 512], F32))
        norm_ps = ctx.enter_context(nc.psum_tensor("norm_ps", [P, 512], F32))
        ada_ps = ctx.enter_context(nc.psum_tensor("ada_ps", [P, 512], F32))
        aux = ctx.enter_context(nc.psum_tensor("aux", [P, 2, 512], F32))

        S = Signals(nc, ctx, totals)
        s_passed = S.passed = S.make("passed")
        s_params_in = S.make("params_in")
        s_lpar_in = S.make("lpar_in")
        s_bcon_in = S.make("bcon_in")
        s_dcon_in = S.make("dcon_in")
        s_x_in = S.make("x_in")
        s_rel_stored = S.make("rel_stored")
        s_hi_made = S.make("hi_made")
        s_lo_made = S.make("lo_made")
        s_mm_done = S.make("mm_done")
        s_evac = S.make("evac")
        s_ada_used = S.make("ada_used")
        s_silu_made = S.make("silu_made")
        s_eps_made = S.make("eps_made")
        s_rel_made = S.make("rel_made")
        s_mods_made = S.make("mods_made")
        s_squared = S.make("squared")
        s_summed = S.make("summed")
        s_r_made = S.make("r_made")
        s_flat_made = S.make("flat_made")
        s_h_hi_made = S.make("h_hi_made")
        s_h_ready = S.make("h_ready")
        s_x_made = S.make("x_made")
        s_gated = S.make("gated")
        s_conved = S.make("conved")
        s_taps_made = S.make("taps_made")
        s_act_made = S.make("act_made")
        s_y_made = S.make("y_made")
        s_evac_y = S.make("evac_y")
        s_scored = S.make("scored")
        s_maxed = S.make("maxed")
        s_exped = S.make("exped")
        s_normed = S.make("normed")
        s_transposed = S.make("transposed")
        s_pt_copied = S.make("pt_copied")
        s_pv_done = S.make("pv_done")
        s_o_hi_made = S.make("o_hi_made")
        s_o_taken = S.make("o_taken")
        s_qkv_made = S.make("qkv_made")
        s_turned_in = S.make("turned_in")
        s_turned = S.make("turned")
        s_logged = S.make("logged")
        s_sp_made = S.make("sp_made")
        s_suffixed = S.make("suffixed")
        s_d_made = S.make("d_made")
        s_w_made = S.make("w_made")
        s_lat_made = S.make("lat_made")
        s_lat_hi_made = S.make("lat_hi_made")
        s_lat_ready = S.make("lat_ready")
        s_v_made = S.make("v_made")
        s_q_turn = S.make("q_turn")
        s_q_turned = S.make("q_turned")
        s_merged = S.make("merged")
        s_merged_hi = S.make("merged_hi")
        s_out_done = S.make("out_done")
        arrived = [ctx.enter_context(nc.semaphore(f"arrived{i}")) for i in range(RAW)]
        ada_in = [ctx.enter_context(nc.semaphore(f"ada_in{i}")) for i in range(2)]
        bias_in = [ctx.enter_context(nc.semaphore(f"bias_in{i}")) for i in range(2)]

        ident = con[:, CCOL["ident"]]
        ones = con[:, CCOL["ones"]]

        def two(ap):
            return ap.rearrange("p (a t) -> p a t", a=2)

        def over(ap, n):
            return ap.unsqueeze(1).to_broadcast([ap.shape[0], n, ap.shape[1]])

        block = ctx.enter_context(nc.Block())

        @block.sync
        def _(eng):
            e = Engine(eng, nc.sync, S)

            def load_chunk(c, slot):
                eng.dma_start(raw[:, slot, :], d["w"][c] if isinstance(c, int) else
                              d["w"][bass.ds(c, 1)].rearrange("o p n -> (o p) n")).then_inc(arrived[slot], 16)

            def load_ada(a, slot):
                eng.dma_start(ada_w[slot][:], d["ada"][a] if isinstance(a, int) else
                              d["ada"][bass.ds(a, 1)].rearrange("o p n -> (o p) n")).then_inc(ada_in[slot], 16)

            def after_chunk(k, k0, turn):
                c = e.chunk(k)
                eng.wait_ge(s_lo_made, c + SPLIT + 1)
                load_chunk(c + SPLIT + RAW, (e.slot(k0) + SPLIT) % RAW)

            def after_ada(a, slot):
                eng.wait_ge(s_ada_used, a + 1)
                load_ada(a + 2, slot)

            def chunks(stage, head=0):
                e.at(stage)
                e.chunks(after_chunk, head)

            eng.dma_start(par[:], d["par"]).then_inc(s_params_in, e.adds(s_params_in, 16))
            for a in range(2):
                load_ada(a, a)
            eng.dma_start(x[:], d["x"]).then_inc(s_x_in, e.adds(s_x_in, 16))
            eng.dma_start(con[:], d["con"]).then_inc(s_params_in, e.adds(s_params_in, 16))
            eng.dma_start(bcon[:], d["bcon"]).then_inc(s_bcon_in, e.adds(s_bcon_in, 16))
            for c in range(SPLIT):
                load_chunk(c, c)
            for a in range(4):
                after_ada(a, a % 2)
            for c in range(SPLIT, RAW):
                load_chunk(c, c)
            for c in range(SPLIT):
                eng.wait_ge(s_lo_made, c + 1)
                load_chunk(c + RAW, c)
            for a in range(4, 8):
                after_ada(a, a % 2)
            chunks("dil_qkv")
            eng.dma_start(dcon[:], d["dcon"]).then_inc(s_dcon_in, e.adds(s_dcon_in, 16))
            for a in range(8, 16):
                after_ada(a, a % 2)
            chunks("na_qkv")
            for a in range(16, 24):
                after_ada(a, a % 2)
            for stage in ("gates1", "branch1", "out1", "up1"):
                chunks(stage)
            chunks("down1", 1)
            with e.layers() as l:
                first = ADA_ONCE + ADA_LAYER * l
                with eng.Fori(0, 4) as i:
                    for j in range(2):
                        after_ada(first + 2 * i + j, j)
                e.at("gateup0")

                def with_ada(k, k0, turn):
                    after_chunk(k, k0, turn)
                    if k0 % 2 == 0:
                        after_ada(first + 8 + 2 * turn + k0 // 2, k0 // 2 % 2)
                e.chunks(with_ada)
                after_ada(first + 19, 1)
                chunks("down0", 1)
                chunks("moba_qkv")
                for a in range(20, 28):
                    after_ada(first + a, a % 2)
                chunks("sb_qkv")
                for a in range(28, 36):
                    after_ada(first + a, a % 2)
                for stage in ("latent", "mla_up", "gates", "branch", "out", "gateup2"):
                    chunks(stage)
                chunks("down2", 1)
            for slot in range(RAW):
                eng.wait_ge(arrived[slot], 16 * len(range(slot, CHUNKS + SPLIT + RAW, RAW)))
            for slot in range(2):
                eng.wait_ge(ada_in[slot], 16 * (ADA_CHUNKS // 2 + 1))
            e.at("end")
            eng.wait_ge(s_x_made, e.past(s_x_made))
            eng.dma_start(d["out"], x[:]).then_inc(s_out_done, e.adds(s_out_done, 16))
            eng.wait_ge(s_out_done, e.past(s_out_done) + 16)

        @block.gpsimd
        def _(eng):
            e = Engine(eng, nc.gpsimd, S)
            nc.gpsimd.memset(eps[:], EPS).then_inc(s_eps_made, e.adds(s_eps_made))

        @block.tensor
        def _(eng):
            e = Engine(eng, nc.tensor, S)
            mm = nc.tensor.matmul

            def three(out, w_hi, w_lo, a_hi, a_lo, start, stop, skip=False):
                mm(out, w_hi, a_hi, start=start, stop=False, skip_group_check=skip)
                mm(out, w_hi, a_lo, start=False, stop=False, skip_group_check=skip)
                return mm(out, w_lo, a_hi, start=False, stop=stop, skip_group_check=skip)

            def ada_chunk(a, slot, turn, col):
                eng.wait_ge(ada_in[slot], 16 * (turn + 1))
                for j in range(2):
                    for k in range(KT):
                        b = j * KT + k
                        out = ada_ps[:, bass.ds(col + j, 1)] if not isinstance(col, int) \
                            else ada_ps[:, col + j:col + j + 1]
                        ins = mm(out, ada_w[slot][:, b * P:(b + 1) * P],
                                 cs[:, a + k:a + k + 1], start=(k == 0), stop=(k == KT - 1))
                ins.then_inc(s_ada_used, e.adds(s_ada_used))

            def ada_once(a):
                ada_chunk(0, a % 2, a // 2, 2 * a)

            def ada_layer(a, a0, turn2):
                first = (ADA_ONCE // 2) + (ADA_LAYER // 2) * e.l
                ada_chunk(8, a0 % 2, first + a0 // 2 + turn2, 2 * a)

            def fm(k, k0, turn):
                c = e.chunk(k)
                s = e.slot(k0) % SPLIT
                if not (isinstance(k, int) and k < 2):
                    eng.wait_ge(s_evac, e.past(s_evac) + k - 1)
                eng.wait_ge(s_lo_made, c + 1)
                for j in range(2):
                    for t in range(KT):
                        if isinstance(k, int) and k == 0 and j == 0 and t % 2 == 0:
                            eng.wait_ge(s_h_ready, e.past(s_h_ready) - 3 + t // 2)
                        b = slice((j * KT + t) * P, (j * KT + t + 1) * P)
                        ins = three(lin[:, k0 % 2, j * SEQ:(j + 1) * SEQ], hi[s][:, b], lo[s][:, b],
                                    h_hi[:, t, :], h_lo[:, t, :], t == 0, t == KT - 1)
                ins.then_inc(s_mm_done, e.adds(s_mm_done))

            def tm(k):
                s = e.slot(k) % SPLIT
                eng.wait_ge(s_evac, e.past(s_evac) + k - 1)
                eng.wait_ge(s_lo_made, e.chunk(k) + 1)
                for j in range(2):
                    for t in range(KT):
                        b = slice(t * SEQ, (t + 1) * SEQ)
                        ins = three(lin[:, k % 2, j * SEQ:(j + 1) * SEQ],
                                    h_hi[:, t, j * P:(j + 1) * P], h_lo[:, t, j * P:(j + 1) * P],
                                    hi[s][:, b], lo[s][:, b], t == 0, t == KT - 1)
                ins.then_inc(s_mm_done, e.adds(s_mm_done))

            def enter(stage):
                e.at(stage)
                eng.wait_ge(s_evac, e.past(s_evac))
                eng.wait_ge(s_evac_y, e.past(s_evac_y))
                eng.wait_ge(s_o_taken, e.past(s_o_taken))

            def sums(stage, n=4):
                e.at(stage)
                for p in range(n):
                    eng.wait_ge(s_squared, e.past(s_squared) + p + 1)
                    for j in range(2):
                        ins = mm(norm_ps[:, 0:SEQ], ones, work[p][:, j, :],
                                 start=(p == 0 and j == 0), stop=(p == n - 1 and j == 1))
                ins.then_inc(s_summed, e.adds(s_summed))

            def down(stage):
                enter(stage)
                eng.wait_ge(s_act_made, e.past(s_act_made))

                def body(k, k0, turn):
                    s = e.slot(k0) % SPLIT
                    eng.wait_ge(s_lo_made, e.chunk(k) + 1)
                    last = isinstance(k, int) and k == FT // 2 - 1
                    for kk in range(2):
                        if isinstance(k, int):
                            a = act_hi[:, 2 * k + kk, :], act_lo[:, 2 * k + kk, :]
                        else:
                            a = [m[:].rearrange("p a t -> p (a t)")[:, bass.ds((2 * k + kk) * SEQ, SEQ)]
                                 for m in (act_hi, act_lo)]
                        for n in range(KT):
                            b = slice((kk * KT + n) * P, (kk * KT + n + 1) * P)
                            first = isinstance(k, int) and k == 0 and kk == 0 and n % 2 == 0
                            ins = three(lin[:, n // 2, (n % 2) * SEQ:(n % 2 + 1) * SEQ],
                                        hi[s][:, b], lo[s][:, b], a[0], a[1],
                                        first, last and kk == 1, skip=True)
                    ins.then_inc(s_mm_done, e.adds(s_mm_done))
                e.chunks(body, head=1)

            def qkv(stage, turn=False):
                enter(stage)
                for k in range(6):
                    if k < 4:
                        fm(k, k, 0)
                    else:
                        tm(k)
                    if turn and 1 <= k <= 4:
                        eng.wait_ge(s_turned_in, e.past(s_turned_in) + k)
                        mm(aux[:, (k - 1) % 2, :], dcon[:, DCOL["rot_p"]],
                                  work[(k - 1) % 2][:].rearrange("p a t -> p (a t)"),
                                  start=True, stop=True).then_inc(s_turned, e.adds(s_turned))

            def attention(stage, q, k, rows, flip, ada=None):
                enter(stage)
                eng.wait_ge(s_qkv_made, e.past(s_qkv_made))
                for i in range(HEADS + 2):
                    if i < HEADS:
                        if i >= 2:
                            eng.wait_ge(s_maxed, e.past(s_maxed) + i - 1)
                        r = rows(i)
                        for t in range(2):
                            ins = mm(lin[:, i % 2, t * SEQ:(t + 1) * SEQ], q(i)[r, t * P:(t + 1) * P],
                                     k(i)[r, :], start=True, stop=flip is None)
                            if flip is not None:
                                if t == 0:
                                    eng.wait_ge(bias_in[i % 2], flip(i))
                                ins = mm(lin[:, i % 2, t * SEQ:(t + 1) * SEQ], bcon[:, BCOL["flip"]],
                                         bias[i % 2][:, t, :], start=False, stop=True)
                        ins.then_inc(s_scored, e.adds(s_scored))
                        if ada is not None:
                            ada(i)
                    h = i - 1
                    if 0 <= h < HEADS:
                        eng.wait_ge(s_normed, e.past(s_normed) + h + 1)
                        if h >= 1:
                            eng.wait_ge(s_pt_copied, e.past(s_pt_copied) + h)
                        for t in range(2):
                            for u in range(2):
                                ins = nc.tensor.transpose(lin[:, 2, u * SEQ + t * P:u * SEQ + (t + 1) * P],
                                                          work[h % 2][:, t, u * P:(u + 1) * P], ident)
                        ins.then_inc(s_transposed, e.adds(s_transposed))
                    values(i - 2, s_pt_copied)

            def values(h, ready):
                if h < 0:
                    return
                eng.wait_ge(ready, e.past(ready) + h + 1)
                if h // 2 >= 2 and h % 2 == 0:
                    eng.wait_ge(s_o_taken, e.past(s_o_taken) + h // 2 - 1)
                for u in range(2):
                    ins = mm(aux[(h % 2) * HD:(h % 2 + 1) * HD, h // 2 % 2, 0:SEQ],
                             v[:, u, h * HD:(h + 1) * HD], work[2 + h % 2][:, u, :],
                             start=(u == 0), stop=(u == 1))
                ins.then_inc(s_pv_done, e.adds(s_pv_done))

            def stick_breaking(stage, ada):
                enter(stage)
                eng.wait_ge(s_qkv_made, e.past(s_qkv_made))
                for i in range(HEADS + 2):
                    if i < HEADS:
                        if i >= 2:
                            eng.wait_ge(s_d_made, e.past(s_d_made) + i - 1)
                        r = slice((i % 2) * HD, (i % 2 + 1) * HD)
                        for u in range(2):
                            ins = mm(lin[:, i % 2, u * SEQ:(u + 1) * SEQ],
                                     kt_[r, i // 2, u * P:(u + 1) * P], qt[r, i // 2, :],
                                     start=(u == 0), stop=(u == 1), skip_group_check=True)
                        ins.then_inc(s_scored, e.adds(s_scored))
                        ada(i)
                    h = i - 1
                    if 0 <= h < HEADS:
                        eng.wait_ge(s_sp_made, e.past(s_sp_made) + h + 1)
                        sp = work[h % 2]
                        bank = lin[:, h % 2, :]
                        mm(bank[:, 0:SEQ], dcon[:, DCOL["neg_tri"]], sp[:, 0, :], start=False, stop=False,
                           skip_group_check=True)
                        mm(bank[:, 0:SEQ], dcon[:, DCOL["neg_ones"]], sp[:, 1, :], start=False, stop=True,
                           skip_group_check=True)
                        mm(bank[:, SEQ:2 * SEQ], dcon[:, DCOL["neg_tri"]], sp[:, 1, :], start=False,
                                  stop=True, skip_group_check=True).then_inc(s_suffixed, e.adds(s_suffixed))
                    values(i - 2, s_w_made)

            def branches(stage, n):
                enter(stage)
                for k in range(2 * n):
                    if k >= 2:
                        eng.wait_ge(s_evac, e.past(s_evac) + k - 1)
                    s = e.slot(k) % SPLIT
                    eng.wait_ge(s_lo_made, e.chunk(k) + 1)
                    for j in range(4):
                        for t in range(4):
                            b = slice((j * 4 + t) * P, (j * 4 + t + 1) * P)
                            bank = 2 * (k % 2) + j // 2
                            ins = three(lin[:, bank, (j % 2) * SEQ:(j % 2 + 1) * SEQ], hi[s][:, b],
                                        lo[s][:, b], br_hi[:, (k // 2) * 4 + t, :],
                                        br_lo[:, (k // 2) * 4 + t, :], t == 0, t == 3)
                    ins.then_inc(s_mm_done, e.adds(s_mm_done))

            def out_proj(stage):
                enter(stage)
                e.chunks(fm)

            def rows64(i):
                return slice((i % 2) * HD, (i % 2 + 1) * HD)

            eng.wait_ge(s_params_in, e.past(s_params_in) + 32)
            eng.wait_ge(s_bcon_in, 16)
            mm(aux[0:HEADS, 0, :], par[0:32, PCOL["rel_bias"]], bcon[0:32, BCOL["onehot"]],
                      start=True, stop=True).then_inc(s_rel_made, e.adds(s_rel_made))
            e.at("ada")
            eng.wait_ge(s_silu_made, e.past(s_silu_made))
            for a in range(8):
                ada_once(a)
            sums("norm1")
            qkv("dil_qkv")
            attention("dil_attn", lambda i: qt[:, i // 2, :], lambda i: kt_[:, i // 2, :], rows64,
                      lambda i: 32 * (i // 2 + 1), ada=lambda i: ada_once(8 + i))
            qkv("na_qkv")
            attention("na_attn", lambda i: qt[:, i // 2, :], lambda i: kt_[:, i // 2, :], rows64,
                      lambda i: 32 * (HEADS // 2) + 64 * (i // 2 + 1), ada=lambda i: ada_once(16 + i))
            enter("gates1")
            e.chunks(fm)
            branches("branch1", 2)
            out_proj("out1")
            sums("norm2")
            enter("up1")
            e.chunks(fm, head=2)
            down("down1")
            sums("norm3")

            with e.layers():
                e.at("ada0")
                eng.wait_ge(s_mods_made, e.past(s_mods_made))
                with e.loop(4) as i:
                    for s in range(2):
                        ada_layer(2 * i + s, s, i)
                sums("pre0")
                enter("gateup0")

                def with_ada(k, k0, turn):
                    fm(k, k0, turn)
                    if k0 % 2 == 0:
                        a0 = 8 + k0 // 2
                        ada_layer(2 * turn + a0, a0, turn)
                e.chunks(with_ada, head=2)
                ada_layer(19, 19, 0)
                down("down0")
                sums("post0")
                sums("pre1")
                qkv("moba_qkv", turn=True)
                attention("moba_attn", lambda i: qt[:, i // 2, :], lambda i: kt_[:, i // 2, :], rows64, None,
                          ada=lambda i: ada_layer(20 + i, 20 + i, 0))
                qkv("sb_qkv")
                stick_breaking("sb_attn", lambda i: ada_layer(28 + i, 28 + i, 0))

                enter("latent")
                fm(0, 0, 0)
                s = e.slot(1) % SPLIT
                eng.wait_ge(s_lo_made, e.chunk(1) + 1)
                for at, m, j in ((0, P, 0), (P, MLA_QK, 1)):
                    for t in range(KT):
                        b = slice(t * 224 + at, t * 224 + at + m)
                        ins = three(lin[0:m, 1, j * SEQ:(j + 1) * SEQ], hi[s][:, b], lo[s][:, b],
                                    h_hi[:, t, :], h_lo[:, t, :], t == 0, t == KT - 1)
                ins.then_inc(s_mm_done, e.adds(s_mm_done))
                eng.wait_ge(s_squared, e.past(s_squared) + 1)
                for j in range(2):
                    mm(norm_ps[:, 0:SEQ], ones, work[2][:, j, :], start=(j == 0), stop=(j == 1))
                eng.wait_ge(s_squared, e.past(s_squared) + 2)
                mm(norm_ps[:, SEQ:2 * SEQ], ones, work[3][:, 0, :], start=True, stop=True).then_inc(s_summed, e.adds(s_summed))
                eng.wait_ge(s_turned_in, e.past(s_turned_in) + 1)
                mm(aux[0:MLA_QK, 0, 0:SEQ], dcon[0:MLA_QK, DCOL["rot_m"]][:, 0:MLA_QK],
                          work[1][0:MLA_QK, 1, :], start=True, stop=True).then_inc(s_turned, e.adds(s_turned))

                enter("mla_up")
                eng.wait_ge(s_lat_ready, e.past(s_lat_ready))
                s = e.slot(0) % SPLIT
                eng.wait_ge(s_lo_made, e.chunk(0) + 1)
                for h in range(HEADS):
                    for t in range(2):
                        b = slice(t * 768 + h * MLA_QK, t * 768 + (h + 1) * MLA_QK)
                        ins = three(lin[0:MLA_QK, h // 2, (h % 2) * SEQ:(h % 2 + 1) * SEQ], hi[s][:, b],
                                    lo[s][:, b], lat_hi[:, t, :], lat_lo[:, t, :], t == 0, t == 1)
                ins.then_inc(s_mm_done, e.adds(s_mm_done))
                def partners(g):
                    eng.wait_ge(s_q_turn, e.past(s_q_turn) + g + 1)
                    if g >= 2:
                        eng.wait_ge(s_evac, e.past(s_evac) + g - 1)
                    mm(aux[0:MLA_QK, g % 2, :], dcon[0:MLA_QK, DCOL["rot_m"]][:, 0:MLA_QK],
                       qm[0:MLA_QK, 2 * g:2 * g + 2, :].rearrange("p a t -> p (a t)"),
                       start=True, stop=True).then_inc(s_q_turned, e.adds(s_q_turned))

                partners(0)
                partners(1)
                s = e.slot(1) % SPLIT
                eng.wait_ge(s_lo_made, e.chunk(1) + 1)
                for h in range(HEADS):
                    if h % 2 == 0:
                        eng.wait_ge(s_q_turn, e.past(s_q_turn) + h // 2 + 1)
                    b = slice(h * MLA_QK, (h + 1) * MLA_QK)
                    three(lin[0:MLA_QK, h // 2, (h % 2) * SEQ:(h % 2 + 1) * SEQ], hi[s][:, b],
                          lo[s][:, b], lat_hi[:, 2, :], lat_lo[:, 2, :], True, True)
                partners(2)
                partners(3)
                eng.wait_ge(s_evac, e.past(s_evac) + 4)
                for u in range(2):
                    ins = three(aux[:, u, :], lat_hi[:, 2, u * P:(u + 1) * P], lat_lo[:, 2, u * P:(u + 1) * P],
                                hi[s][:, 768:1280], lo[s][:, 768:1280], True, True)
                ins.then_inc(s_mm_done, e.adds(s_mm_done))
                attention("mla_attn", lambda i: qm[:, i, :], lambda i: km[:, i, :],
                          lambda i: slice(0, MLA_QK), None)
                enter("gates")
                e.chunks(fm)
                branches("branch", 3)
                out_proj("out")
                sums("out")
                sums("pre2")
                enter("gateup2")
                e.chunks(fm, head=2)
                down("down2")
                sums("post2")

        @block.scalar
        def _(eng):
            e = Engine(eng, nc.scalar, S)
            act = nc.scalar.activation

            def split(c, slot, turn):
                eng.wait_ge(arrived[slot], 16 * (turn + 1))
                if not isinstance(c, int) or c >= SPLIT:
                    eng.wait_ge(s_mm_done, c - (SPLIT - 1))
                act(hi[slot % SPLIT][:], raw[:, slot, :], ACT.Copy).then_inc(s_hi_made, e.adds(s_hi_made))

            def later_split(k, k0, turn):
                split(e.chunk(k) + SPLIT, e.slot(k0 + SPLIT), e.round(k0 + SPLIT, turn))

            def log_exp():
                nc.scalar.preload_act_table_set("natural_log_exp_and_others")

            def squares(src, ready):
                for p in range(4):
                    if ready is not None:
                        ready(p)
                    act(work[p][:], src(p), ACT.Square).then_inc(s_squared, e.adds(s_squared))

            def rsqrt(width=1.0 / D):
                log_exp()
                eng.wait_ge(s_summed, e.past(s_summed) + 1)
                act(rs[:, 0, :], norm_ps[:, 0:SEQ], ACT.Ln, bias=eps[:, 0:1], scale=width)
                nc.scalar.drain()
                act(rs[:, 0, :], rs[:, 0, :], ACT.Exp, scale=-0.5).then_inc(s_r_made, e.adds(s_r_made))

            def pre_norm(stage):
                e.at(stage)
                eng.wait_ge(s_x_made, e.past(s_x_made))
                squares(lambda p: x[:, 2 * p:2 * p + 2, :], None)
                rsqrt()
                for p in range(4):
                    eng.wait_ge(s_flat_made, e.past(s_flat_made) + p + 1)
                    act(h_hi[:, 2 * p:2 * p + 2, :], flat[:, 2 * p:2 * p + 2, :], ACT.Copy).then_inc(s_h_hi_made, e.adds(s_h_hi_made))

            def lin_stage(stage, first=None, second=None, head=0):
                e.at(stage)

                def body(k, k0, turn):
                    if first is not None:
                        first(k, k0)
                    later_split(k, k0, turn)
                    if second is not None:
                        second(k, k0)
                e.chunks(body, head)

            def wait_mm(k):
                eng.wait_ge(s_mm_done, e.chunk(k) + 1)

            def o_hi(i, br):
                h = i - 3
                if h >= 0 and h % 2 == 1:
                    eng.wait_ge(s_pv_done, e.past(s_pv_done) + h + 1)
                    n = h // 2
                    act(br_hi[:, 4 * br + n, :], aux[:, n % 2, 0:SEQ], ACT.Copy).then_inc(s_o_hi_made, e.adds(s_o_hi_made))

            def load_bias(kind, i):
                b = bias[i % 2]
                for t in range(2):
                    if kind == "dil":
                        src = bass.AP(d["rel"].tensor, i * 2 * SEQ + P * (1 - t), [[1, P], [1, SEQ]])
                        eng.dma_start(b[:, t, :], src).then_inc(bias_in[i % 2], 16)
                    else:
                        for r in range(2):
                            at = i * N_RPB + (6 - 2 * t + r) * 31 - 48
                            src = bass.AP(d["rpb"].tensor, at, [[1, GRID_W], [31, ROWS], [1, GRID_W]])
                            dst = b[r * GRID_W:(r + 1) * GRID_W, t, :].rearrange("p (a c) -> p a c", a=ROWS)
                            eng.dma_start(dst, src).then_inc(bias_in[i % 2], 16)

            def attention(stage, br, kind=None):
                e.at(stage)
                log_exp()
                for i in range(HEADS + 4):
                    if i < HEADS:
                        eng.wait_ge(s_maxed, e.past(s_maxed) + i + 1)
                        if kind is not None and i + 2 < HEADS:
                            load_bias(kind, i + 2)
                        for t in range(2):
                            ins = act(work[i % 2][:, t, :], work[i % 2][:, t, :], ACT.Exp,
                                      bias=neg_mx[:, i % 2, t:t + 1], accum_out=den[:, i % 2, t:t + 1])
                        ins.then_inc(s_exped, e.adds(s_exped))
                    h = i - 1
                    if 0 <= h < HEADS:
                        eng.wait_ge(s_transposed, e.past(s_transposed) + h + 1)
                        act(work[2 + h % 2][:], two(lin[:, 2, :]), ACT.Copy).then_inc(s_pt_copied, e.adds(s_pt_copied))
                    o_hi(i, br)

            def stick_breaking(stage, br):
                e.at(stage)
                log_exp()
                for i in range(HEADS + 4):
                    if i < HEADS:
                        eng.wait_ge(s_scored, e.past(s_scored) + i + 1)
                        w = work[i % 2][:]
                        act(w, two(lin[:, i % 2, :]), ACT.Abs)
                        nc.scalar.drain()
                        act(w, w, ACT.Exp, scale=-1.0)
                        nc.scalar.drain()
                        act(w, w, ACT.Ln, bias=1.0).then_inc(s_logged, e.adds(s_logged))
                    h = i - 1
                    if 0 <= h < HEADS:
                        eng.wait_ge(s_d_made, e.past(s_d_made) + h + 1)
                        act(work[2 + h % 2][:], work[2 + h % 2][:], ACT.Exp).then_inc(s_w_made, e.adds(s_w_made))
                    o_hi(i, br)

            def silu_gate(k, k0):
                wait_mm(k)
                act(work[2 + k0 % 2][:, 0, :], lin[:, k0 % 2, 0:SEQ], ACT.Silu).then_inc(s_gated, e.adds(s_gated))

            def conv_mid(k, k0):
                wait_mm(k)
                for j in range(2):
                    at = PCOL["conv"].start + 4 * j
                    ins = act(work[k0 % 2][:, j, :], lin[:, k0 % 2, j * SEQ:(j + 1) * SEQ], ACT.Identity,
                              bias=par[:, bass.ds(8 * k + (at + 3), 1)], scale=par[:, bass.ds(8 * k + (at + 1), 1)])
                ins.then_inc(s_conved, e.adds(s_conved))

            def conv_gate(k, k0):
                eng.wait_ge(s_taps_made, e.past(s_taps_made) + k + 1)
                act(work[2 + k0 % 2][:, 0, :], work[k0 % 2][:, 1, :], ACT.Gelu_apprx_tanh).then_inc(s_gated, e.adds(s_gated))

            def sigmoid_gates(b):
                def evac(k, k0):
                    wait_mm(k)
                    for j in range(2):
                        if isinstance(k, int):
                            out = gates[:, 2 * k + j, :]
                            bb = 0.0 if b is None else lpar[:, b + 2 * k + j:b + 2 * k + j + 1]
                        else:
                            out = gates[:].rearrange("p a t -> p (a t)")[:, bass.ds((2 * k + j) * SEQ, SEQ)]
                            bb = 0.0 if b is None else lpar[:, bass.ds(2 * k + (b + j), 1)]
                        ins = act(out, lin[:, k0 % 2, j * SEQ:(j + 1) * SEQ], ACT.Sigmoid, bias=bb)
                    ins.then_inc(s_evac, e.adds(s_evac))
                return evac

            def merged_hi(last):
                def evac(k, k0):
                    if k >= last:
                        half = k - last
                        eng.wait_ge(s_merged, e.past(s_merged) + k - 1)
                        act(h_hi[:, 4 * half:4 * half + 4, :], flat[:, 4 * half:4 * half + 4, :], ACT.Copy).then_inc(s_merged_hi, e.adds(s_merged_hi))
                return evac

            def post_squares(stage):
                e.at(stage)
                squares(lambda p: flat[:, 2 * p:2 * p + 2, :], lambda p: eng.wait_ge(s_y_made, e.past(s_y_made) + p + 1))
                rsqrt()

            eng.wait_ge(s_params_in, e.past(s_params_in) + 32)
            act(cs[:, 0:16], par[:, 0:16], ACT.Silu).then_inc(s_silu_made, e.adds(s_silu_made))
            eng.wait_ge(s_rel_made, e.past(s_rel_made) + 1)
            act(rel_tab[:], aux[0:HEADS, 0, :], ACT.Copy)
            nc.scalar.drain()
            eng.dma_start(d["rel"], rel_tab[:]).then_inc(s_rel_stored, e.adds(s_rel_stored, 16))
            eng.wait_ge(s_rel_stored, e.past(s_rel_stored) + 16)
            load_bias("dil", 0)
            load_bias("dil", 1)
            for c in range(SPLIT):
                split(c, c, 0)

            e.at("norm1")
            eng.wait_ge(s_x_in, e.past(s_x_in))
            squares(lambda p: x[:, 2 * p:2 * p + 2, :], None)
            eng.wait_ge(s_eps_made, e.past(s_eps_made))
            rsqrt()
            for p in range(4):
                eng.wait_ge(s_flat_made, e.past(s_flat_made) + p + 1)
                act(h_hi[:, 2 * p:2 * p + 2, :], flat[:, 2 * p:2 * p + 2, :], ACT.Copy).then_inc(s_h_hi_made, e.adds(s_h_hi_made))
            lin_stage("dil_qkv", None)
            attention("dil_attn", 0, "dil")
            load_bias("na", 0)
            load_bias("na", 1)
            lin_stage("na_qkv", None)
            attention("na_attn", 1, "na")
            lin_stage("gates1", sigmoid_gates(None))
            lin_stage("branch1", None, merged_hi(2))
            lin_stage("out1", None)
            pre_norm("norm2")
            lin_stage("up1", conv_mid, conv_gate)
            lin_stage("down1", None, head=1)
            e.at("norm3")
            eng.wait_ge(s_x_made, e.past(s_x_made))
            squares(lambda p: x[:, 2 * p:2 * p + 2, :], None)
            rsqrt()

            with e.layers() as l:
                e.at("ada0")
                eng.wait_ge(s_x_made, e.past(s_x_made))
                eng.dma_start(lpar[:], d["lpar"][bass.ds(l, 1)].rearrange("o p n -> (o p) n")).then_inc(s_lpar_in, e.adds(s_lpar_in, 16))
                pre_norm("pre0")
                lin_stage("gateup0", silu_gate)
                lin_stage("down0", None, head=1)
                post_squares("post0")
                pre_norm("pre1")
                lin_stage("moba_qkv", None)
                attention("moba_attn", 0)
                lin_stage("sb_qkv", None)
                stick_breaking("sb_attn", 1)

                def latent(k, k0):
                    eng.wait_ge(s_y_made, e.past(s_y_made) + k + 1)
                    if k == 0:
                        act(work[2][:], work[0][:], ACT.Square).then_inc(s_squared, e.adds(s_squared))
                    else:
                        act(work[3][:, 0, :], work[1][:, 0, :], ACT.Square).then_inc(s_squared, e.adds(s_squared))
                lin_stage("latent", latent)
                eng.wait_ge(s_summed, e.past(s_summed) + 1)
                act(rs[:, 0, :], norm_ps[:, 0:SEQ], ACT.Ln, bias=eps[:, 0:1], scale=1.0 / 256)
                act(rs[:, 1, :], norm_ps[:, SEQ:2 * SEQ], ACT.Ln, bias=eps[:, 0:1], scale=1.0 / 128)
                nc.scalar.drain()
                act(rs[:], rs[:], ACT.Exp, scale=-0.5).then_inc(s_r_made, e.adds(s_r_made))
                eng.wait_ge(s_lat_made, e.past(s_lat_made) + 1)
                act(lat_hi[:, 0:2, :], work[0][:], ACT.Copy).then_inc(s_lat_hi_made, e.adds(s_lat_hi_made))
                act(lat_hi[:, 2, :], work[1][:, 0, :], ACT.Copy).then_inc(s_lat_hi_made, e.adds(s_lat_hi_made))
                def mla_up(k, k0):
                    wait_mm(k)
                    if k == 0:
                        for g in range(4):
                            act(qm[0:MLA_QK, 2 * g:2 * g + 2, :], two(lin[0:MLA_QK, g, :]), ACT.Copy,
                                scale=MLA_QK ** -0.5).then_inc(s_q_turn, e.adds(s_q_turn))
                    else:
                        for u in range(2):
                            act(v[:, u, :], aux[:, u, :], ACT.Copy).then_inc(s_v_made, e.adds(s_v_made))
                lin_stage("mla_up", mla_up)
                attention("mla_attn", 2)
                lin_stage("gates", sigmoid_gates(LCOL["b_gate"].start))
                lin_stage("branch", None, merged_hi(4))

                def y_squares(k, k0):
                    wait_mm(k)
                    act(work[k][:], two(lin[:, k0 % 2, :]), ACT.Square).then_inc(s_squared, e.adds(s_squared))
                lin_stage("out", y_squares)
                rsqrt()
                pre_norm("pre2")
                lin_stage("gateup2", silu_gate)
                lin_stage("down2", None, head=1)
                post_squares("post2")

        @block.vector
        def _(eng):
            e = Engine(eng, nc.vector, S)
            ve = nc.vector
            tt, ts, stt = ve.tensor_tensor, ve.tensor_scalar, ve.scalar_tensor_tensor

            def split(c, slot):
                eng.wait_ge(s_hi_made, c + 1)
                tt(lo[slot % SPLIT][:], raw[:, slot, :], hi[slot % SPLIT][:].bitcast(F32), ALU.subtract).then_inc(s_lo_made, e.adds(s_lo_made))

            def lin_stage(stage, first=None, second=None, head=0):
                e.at(stage)

                def body(k, k0, turn):
                    if first is not None:
                        first(k, k0)
                    split(e.chunk(k) + SPLIT, e.slot(k0 + SPLIT))
                    if second is not None:
                        second(k, k0)
                e.chunks(body, head)

            def wait_mm(k):
                eng.wait_ge(s_mm_done, e.chunk(k) + 1)

            def modulated(gain_, shift):
                eng.wait_ge(s_r_made, e.past(s_r_made) + 1)

                def rest(p):
                    eng.wait_ge(s_h_hi_made, e.past(s_h_hi_made) + p + 1)
                    s = slice(2 * p, 2 * p + 2)
                    tt(h_lo[:, s, :], flat[:, s, :], h_hi[:, s, :].bitcast(F32), ALU.subtract).then_inc(s_h_ready, e.adds(s_h_ready))

                for p in range(4):
                    s = slice(2 * p, 2 * p + 2)
                    tt(flat[:, s, :], x[:, s, :], over(rs[:, 0, :], 2), ALU.mult)
                    ve.drain()
                    for t in range(2 * p, 2 * p + 2):
                        ins = ts(flat[:, t, :], flat[:, t, :], gain_[:, t:t + 1], shift[:, t:t + 1], ALU.mult, ALU.add)
                    ins.then_inc(s_flat_made, e.adds(s_flat_made))
                    if p:
                        rest(p - 1)
                rest(3)

            def residual(s):
                eng.wait_ge(s_r_made, e.past(s_r_made) + 1)
                for p in range(4):
                    a = slice(2 * p, 2 * p + 2)
                    tt(flat[:, a, :], flat[:, a, :], over(rs[:, 0, :], 2), ALU.mult)
                    ve.drain()
                    for t in range(2 * p, 2 * p + 2):
                        ins = stt(x[:, t, :], flat[:, t, :], post_gain[:, 8 * s + t:8 * s + t + 1], x[:, t, :],
                                  ALU.mult, ALU.add)
                    ins.then_inc(s_x_made, e.adds(s_x_made))

            def post(stage, s):
                e.at(stage)
                eng.wait_ge(s_mm_done, e.chunk(0))
                for p in range(4):
                    ve.tensor_copy(flat[:, 2 * p:2 * p + 2, :], two(lin[:, p, :])).then_inc(s_y_made, e.adds(s_y_made))
                ve.drain().then_inc(s_evac_y, e.adds(s_evac_y))
                residual(s)

            def shift_and_gain(s):
                a = 24 * s
                tt(mod[:, a:a + 16], ada_ps[:, a:a + 16], lpar[:, a:a + 16], ALU.add)
                ve.drain()
                g = LCOL["norm_pre"].start + 8 * s
                stt(gain[:, 8 * s:8 * s + 8], mod[:, a + 8:a + 16], 1.0, lpar[:, g:g + 8], ALU.add,
                    ALU.mult).then_inc(s_mods_made, e.adds(s_mods_made))
                ve.drain()

            def gate_gain(s):
                a = 24 * s + 16
                tt(mod[:, a:a + 8], ada_ps[:, a:a + 8], lpar[:, a:a + 8], ALU.add)
                ve.drain()
                g = LCOL["norm_post"].start + 8 * s
                out = post_gain[:, 8 * s:8 * s + 8]
                stt(out, mod[:, a:a + 8], 1.0, lpar[:, g:g + 8], ALU.add, ALU.mult)
                ve.drain()
                ts(out, out, 1.0 if s == 1 else 0.5, None, ALU.mult).then_inc(s_mods_made, e.adds(s_mods_made))
                ve.drain()

            def qkv(stage, turn=False):
                def evac(k, k0):
                    wait_mm(k)
                    bank = two(lin[:, k % 2, :])
                    scale = HD ** -0.5 if k < 2 else 1.0
                    dst = [qt, qt, kt_, kt_][k][:, 2 * (k % 2):2 * (k % 2) + 2, :] if k < 4 else None
                    if k < 4 and not turn:
                        ts(dst, bank, scale, None, ALU.mult).then_inc(s_evac, e.adds(s_evac))
                    elif k < 4:
                        ins = ts(work[k % 2][:], bank, scale, None, ALU.mult).then_inc(s_evac, e.adds(s_evac))
                        ve.drain()
                        ve.tensor_copy(dst, work[k % 2][:]).then_inc(s_turned_in, e.adds(s_turned_in))
                    else:
                        dst = v[:, :, (k - 4) * SEQ:(k - 3) * SEQ]
                        ve.tensor_copy(dst, bank).then_inc(s_evac, e.adds(s_evac))

                def rotate(k, k0):
                    if turn and 1 <= k <= 4:
                        j = k - 1
                        dst = [qt, qt, kt_, kt_][j][:, 2 * (j % 2):2 * (j % 2) + 2, :]
                        eng.wait_ge(s_turned, e.past(s_turned) + j + 1)
                        tt(work[2][:], two(aux[:, j % 2, :]), over(dcon[:, DCOL["sin_p"]], 2), ALU.mult)
                        tt(dst, dst, over(dcon[:, DCOL["cos_p"]], 2), ALU.mult)
                        ve.drain()
                        tt(dst, dst, work[2][:], ALU.add)
                        ve.drain()
                lin_stage(stage, evac, rotate)
                ve.drain().then_inc(s_qkv_made, e.adds(s_qkv_made))

            def o_lo(i, br):
                h = i - 3
                if h >= 0 and h % 2 == 1:
                    n = h // 2
                    eng.wait_ge(s_o_hi_made, e.past(s_o_hi_made) + n + 1)
                    tt(br_lo[:, 4 * br + n, :], aux[:, n % 2, 0:SEQ],
                              br_hi[:, 4 * br + n, :].bitcast(F32), ALU.subtract).then_inc(s_o_taken, e.adds(s_o_taken))

            def attention(stage, br, mask):
                e.at(stage)
                for i in range(HEADS + 4):
                    if i < HEADS:
                        eng.wait_ge(s_scored, e.past(s_scored) + i + 1)
                        if e.in_layers():
                            eng.sem_inc(s_passed, 1)
                        for t in range(2):
                            ve.tensor_tensor_reduce(out=work[i % 2][:, t, :], in0=lin[:, i % 2, t * SEQ:(t + 1) * SEQ],
                                                    in1=mask[:, t * SEQ:(t + 1) * SEQ], scale=1.0, scalar=-3e38,
                                                    op0=ALU.add, op1=ALU.max, accum_out=mx[:, i % 2, t:t + 1])
                        ve.drain()
                        ts(neg_mx[:, i % 2, :], mx[:, i % 2, :], -1.0, None, ALU.mult).then_inc(s_maxed, e.adds(s_maxed))
                    h = i - 1
                    if 0 <= h < HEADS:
                        eng.wait_ge(s_exped, e.past(s_exped) + h + 1)
                        ve.reciprocal(rden[:, h % 2, :], den[:, h % 2, :])
                        ve.drain()
                        for t in range(2):
                            ins = ts(work[h % 2][:, t, :], work[h % 2][:, t, :], rden[:, h % 2, t:t + 1], None,
                                     ALU.mult)
                        ins.then_inc(s_normed, e.adds(s_normed))
                    o_lo(i, br)

            def stick_breaking(stage, br):
                e.at(stage)
                for i in range(HEADS + 4):
                    if i < HEADS:
                        eng.wait_ge(s_logged, e.past(s_logged) + i + 1)
                        w = work[i % 2][:]
                        stt(w, two(lin[:, i % 2, :]), 0.0, w, ALU.max, ALU.add)
                        ve.drain()
                        tt(w, w, two(dcon[:, DCOL["sb_mul"]]), ALU.mult).then_inc(s_sp_made, e.adds(s_sp_made))
                    h = i - 1
                    if 0 <= h < HEADS:
                        eng.wait_ge(s_suffixed, e.past(s_suffixed) + h + 1)
                        tt(work[2 + h % 2][:], two(lin[:, h % 2, :]), two(dcon[:, DCOL["sb_add"]]), ALU.add).then_inc(s_d_made, e.adds(s_d_made))
                    o_lo(i, br)

            def split_act(k, a):
                sides = [m[:].rearrange("p a t -> p (a t)")[:, bass.ds(k * SEQ, SEQ)] if not isinstance(k, int)
                         else m[:, k, :] for m in (act_hi, act_lo)]
                ve.tensor_copy(sides[0], a)
                ve.drain()
                return tt(sides[1], a, sides[0].bitcast(F32), ALU.subtract)

            def swiglu(k, k0):
                eng.wait_ge(s_gated, e.past(s_gated) + k + 1)
                w = work[2 + k0 % 2]
                tt(w[:, 1, :], w[:, 0, :], lin[:, k0 % 2, SEQ:2 * SEQ], ALU.mult).then_inc(s_evac, e.adds(s_evac))

            def hidden(k, k0):
                ve.drain()
                split_act(k, work[2 + k0 % 2][:, 1, :]).then_inc(s_act_made, e.adds(s_act_made))

            def conv_taps(k, k0):
                eng.wait_ge(s_conved, e.past(s_conved) + k + 1)
                for j in (1, 0):
                    at = PCOL["conv"].start + 4 * j
                    u = work[k0 % 2][:, j, :]
                    p = lin[:, k0 % 2, j * SEQ:(j + 1) * SEQ]
                    stt(u[:, 1:SEQ], p[:, 0:SEQ - 1], par[:, bass.ds(8 * k + at, 1)], u[:, 1:SEQ], ALU.mult, ALU.add)
                    ve.drain()
                    ins = stt(u[:, 0:SEQ - 1], p[:, 1:SEQ], par[:, bass.ds(8 * k + (at + 2), 1)], u[:, 0:SEQ - 1],
                              ALU.mult, ALU.add)
                    ins.then_inc((s_taps_made if j == 1 else s_evac), e.adds((s_taps_made if j == 1 else s_evac)))

            def conv_glu(k, k0):
                ve.drain()
                eng.wait_ge(s_gated, e.past(s_gated) + k + 1)
                w = work[2 + k0 % 2]
                tt(w[:, 1, :], w[:, 0, :], work[k0 % 2][:, 0, :], ALU.mult)
                ve.drain()
                split_act(k, w[:, 1, :]).then_inc(s_act_made, e.adds(s_act_made))

            def merge(k, k0):
                wait_mm(k)
                n, half = k // 2, k % 2
                a = slice(4 * half, 4 * half + 4)
                g = gates[:, 8 * n + 4 * half:8 * n + 4 * half + 4, :]
                y = lin[:, 2 * half:2 * half + 2, :].rearrange("p b (a t) -> p (b a) t", a=2)
                if n == 0:
                    tt(flat[:, a, :], g, y, ALU.mult).then_inc(s_evac, e.adds(s_evac))
                else:
                    tt(g, g, y, ALU.mult).then_inc(s_evac, e.adds(s_evac))
                    ve.drain()
                    tt(flat[:, a, :], flat[:, a, :], g, ALU.add).then_inc(s_merged, e.adds(s_merged))

            def merged_lo(last):
                def rest(k, k0):
                    if k >= last:
                        half = k % 2
                        a = slice(4 * half, 4 * half + 4)
                        eng.wait_ge(s_merged_hi, e.past(s_merged_hi) + half + 1)
                        tt(h_lo[:, a, :], flat[:, a, :], h_hi[:, a, :].bitcast(F32),
                           ALU.subtract).then_inc(s_h_ready, e.adds(s_h_ready, 2))
                return rest

            eng.wait_ge(s_params_in, e.past(s_params_in) + 32)
            for c in range(SPLIT):
                split(c, c)
            e.at("ada")
            eng.wait_ge(s_ada_used, e.past(s_ada_used) + 8)
            tt(mod[:, 0:16], ada_ps[:, 0:16], par[:, PCOL["b_ada"]][:, 0:16], ALU.add)
            ve.drain()
            stt(gain[:, 0:8], mod[:, 8:16], 1.0, par[:, PCOL["g_mix"]], ALU.add, ALU.mult)
            ve.drain()
            e.at("norm1")
            modulated(gain, mod)
            qkv("dil_qkv")
            eng.wait_ge(s_bcon_in, e.past(s_bcon_in))
            attention("dil_attn", 0, bcon[:, BCOL["dil"]])
            qkv("na_qkv")
            attention("na_attn", 1, bcon[:, BCOL["na"]])
            lin_stage("gates1", None)
            lin_stage("branch1", merge, merged_lo(2))
            e.at("mods1")
            eng.wait_ge(s_ada_used, e.past(s_ada_used))
            tt(mod[:, 16:48], ada_ps[:, 16:48], par[:, PCOL["b_ada"]][:, 16:48], ALU.add)
            ve.drain()
            stt(gain[:, 8:16], mod[:, 32:40], 1.0, par[:, PCOL["g_ffn"]], ALU.add, ALU.mult)
            ve.drain().then_inc(s_mods_made, e.adds(s_mods_made))

            def out_residual(k, k0):
                wait_mm(k)
                for j in range(2):
                    t = 2 * k + j
                    ins = stt(x[:, t, :], lin[:, k0 % 2, j * SEQ:(j + 1) * SEQ], mod[:, 16 + t:17 + t], x[:, t, :],
                              ALU.mult, ALU.add)
                ins.then_inc(s_evac, e.adds(s_evac))
                if k == 3:
                    ve.drain().then_inc(s_x_made, e.adds(s_x_made))
            lin_stage("out1", out_residual)
            e.at("norm2")
            modulated(gain[:, 8:16], mod[:, 24:32])
            lin_stage("up1", conv_taps, conv_glu)
            lin_stage("down1", None, head=1)
            eng.wait_ge(s_mm_done, e.chunk(FT // 2))
            for t in range(KT):
                ins = stt(x[:, t, :], lin[:, t // 2, (t % 2) * SEQ:(t % 2 + 1) * SEQ], mod[:, 40 + t:41 + t],
                          x[:, t, :], ALU.mult, ALU.add)
            ins.then_inc(s_evac, e.adds(s_evac))
            ve.drain().then_inc(s_x_made, e.adds(s_x_made))
            e.at("norm3")
            eng.wait_ge(s_r_made, e.past(s_r_made) + 1)
            tt(flat[:], x[:], over(rs[:, 0, :], KT), ALU.mult)
            ve.drain()
            g = PCOL["g_final"].start
            for t in range(KT):
                ins = ts(x[:, t, :], flat[:, t, :], par[:, g + t:g + t + 1], None, ALU.mult)
            ins.then_inc(s_x_made, e.adds(s_x_made))

            with e.layers():
                e.at("ada0")
                eng.wait_ge(s_lpar_in, e.past(s_lpar_in) + 16)
                eng.wait_ge(s_ada_used, e.past(s_ada_used) + 8)
                shift_and_gain(0)
                e.at("pre0")
                modulated(gain[:, 0:8], mod[:, 0:8])
                lin_stage("gateup0", swiglu, hidden)
                eng.wait_ge(s_ada_used, e.past(s_ada_used) + 12)
                gate_gain(0)
                shift_and_gain(1)
                lin_stage("down0", None, head=1)
                post("post0", 0)
                e.at("pre1")
                modulated(gain[:, 8:16], mod[:, 24:32])
                eng.wait_ge(s_dcon_in, e.past(s_dcon_in))
                qkv("moba_qkv", turn=True)
                attention("moba_attn", 0, con[:, CCOL["causal"]])
                qkv("sb_qkv")
                stick_breaking("sb_attn", 1)
                eng.wait_ge(s_ada_used, e.past(s_ada_used) + 8)
                gate_gain(1)
                shift_and_gain(2)
                gate_gain(2)

                def latent(k, k0):
                    wait_mm(k)
                    if k == 0:
                        ve.tensor_copy(work[0][:], two(lin[:, 0, :])).then_inc(s_y_made, e.adds(s_y_made))
                    else:
                        ve.tensor_copy(work[1][:, 0, :], lin[:, 1, 0:SEQ]).then_inc(s_y_made, e.adds(s_y_made))
                        ve.tensor_copy(work[1][0:MLA_QK, 1, :], lin[0:MLA_QK, 1, SEQ:2 * SEQ]).then_inc(s_turned_in, e.adds(s_turned_in))
                lin_stage("latent", latent)
                eng.wait_ge(s_turned, e.past(s_turned) + 1)
                kr = work[1][0:MLA_QK, 1, :]
                rot = work[3][0:MLA_QK, 1, :]
                tt(rot, aux[0:MLA_QK, 0, 0:SEQ], dcon[0:MLA_QK, DCOL["sin_m"]], ALU.mult)
                tt(kr, kr, dcon[0:MLA_QK, DCOL["cos_m"]], ALU.mult)
                ve.drain()
                tt(kr, kr, rot, ALU.add)
                eng.wait_ge(s_r_made, e.past(s_r_made) + 1)
                tt(work[0][:], work[0][:], over(rs[:, 0, :], 2), ALU.mult)
                tt(work[1][:, 0, :], work[1][:, 0, :], rs[:, 1, :], ALU.mult)
                ve.drain()
                for t in range(2):
                    q = LCOL["q_norm"].start + t
                    ts(work[0][:, t, :], work[0][:, t, :], lpar[:, q:q + 1], None, ALU.mult)
                q = LCOL["kv_norm"].start
                ts(work[1][:, 0, :], work[1][:, 0, :], lpar[:, q:q + 1], None, ALU.mult).then_inc(s_lat_made, e.adds(s_lat_made))
                eng.wait_ge(s_squared, e.past(s_squared) + 2)
                eng.wait_ge(s_lat_hi_made, e.past(s_lat_hi_made) + 2)
                tt(lat_lo[:, 0:2, :], work[0][:], lat_hi[:, 0:2, :].bitcast(F32), ALU.subtract)
                tt(lat_lo[:, 2, :], work[1][:, 0, :], lat_hi[:, 2, :].bitcast(F32), ALU.subtract).then_inc(s_lat_ready, e.adds(s_lat_ready))
                ve.drain().then_inc(s_evac, e.adds(s_evac))

                def mla_up(k, k0):
                    wait_mm(k)
                    if k == 0:
                        for g in range(4):
                            eng.wait_ge(s_q_turned, e.past(s_q_turned) + g + 1)
                            q = qm[0:MLA_QK, 2 * g:2 * g + 2, :]
                            rot = work[2 + g % 2][0:MLA_QK, :, :]
                            tt(rot, two(aux[0:MLA_QK, g % 2, :]), over(dcon[0:MLA_QK, DCOL["sin_m"]], 2), ALU.mult).then_inc(s_evac, e.adds(s_evac))
                            tt(q, q, over(dcon[0:MLA_QK, DCOL["cos_m"]], 2), ALU.mult)
                            ve.drain()
                            tt(q, q, rot, ALU.add)
                    else:
                        for g in range(4):
                            if g == 3:
                                eng.wait_ge(s_v_made, e.past(s_v_made) + 2)
                            ins = tt(km[0:MLA_QK, 2 * g:2 * g + 2, :], two(lin[0:MLA_QK, g, :]), over(kr, 2), ALU.add)
                        ins.then_inc(s_evac, e.adds(s_evac))
                        ve.drain().then_inc(s_qkv_made, e.adds(s_qkv_made))
                lin_stage("mla_up", mla_up)
                attention("mla_attn", 2, con[:, CCOL["causal"]])
                lin_stage("gates", None)
                lin_stage("branch", merge, merged_lo(4))

                def take_y(k, k0):
                    wait_mm(k)
                    eng.wait_ge(s_squared, e.past(s_squared) + k + 1)
                    ve.tensor_copy(flat[:, 2 * k:2 * k + 2, :], two(lin[:, k0 % 2, :])).then_inc(s_evac, e.adds(s_evac))
                lin_stage("out", take_y)
                residual(1)
                e.at("pre2")
                modulated(gain[:, 16:24], mod[:, 48:56])
                lin_stage("gateup2", swiglu, hidden)
                lin_stage("down2", None, head=1)
                post("post2", 2)
    return S.seen


def constants():
    f = np.float32
    t = np.arange(SEQ)
    con = np.zeros((P, NCCOL), f)
    con[:, CCOL["ident"]] = np.eye(P)
    con[:, CCOL["ones"]] = 1.0

    def by_query(allowed_log):
        return allowed_log.reshape(2, P, SEQ).transpose(1, 0, 2).reshape(P, 2 * SEQ)

    q, k = t[:, None], t[None, :]
    con[:, CCOL["causal"]] = by_query(np.where(k <= q, 0.0, MASKED))

    b = np.zeros((P, NBCOL), f)
    b[:, BCOL["flip"]] = np.eye(P)[::-1]
    delta = k - q
    count = (np.abs(delta) <= 64) * 1 + (delta % 4 == 0) * 1 + (delta % 16 == 0) * 1
    b[:, BCOL["dil"]] = by_query(np.where(count > 0, np.log(np.maximum(count, 1)), MASKED))
    cq, ck = q % GRID_W, k % GRID_W
    start = np.clip(cq - 8, 0, GRID_W - 16)
    b[:, BCOL["na"]] = by_query(np.where((ck >= start) & (ck < start + 16), 0.0, MASKED))
    rel = np.arange(-(SEQ - 1), SEQ + 1)
    a = np.abs(rel)
    large = 8 + (np.log(np.maximum(a, 1).astype(f) / 8) / f(np.log(1024 / 8)) * 8).astype(np.int32)
    bucket = np.where(rel > 0, 16, 0) + np.where(a < 8, a, np.minimum(large, 15))
    b[0:32, BCOL["onehot"]] = bucket[None, :] == np.arange(32)[:, None]

    c = np.zeros((P, NDCOL), f)
    j, i = np.arange(P)[:, None], np.arange(P)[None, :]
    c[:, DCOL["neg_tri"]] = np.where(j >= i, -1.0, 0.0)
    c[:, DCOL["neg_ones"]] = -1.0

    def rotary(n_rot, at, width, rot, cos, sin):
        inv = (f(500000.0) ** (-np.arange(0, n_rot, 2, dtype=f) / n_rot)).astype(f)
        ang = t.astype(f)[:, None] * inv[None, :]
        half = n_rot // 2
        m = np.zeros((P, P), f)
        cc, ss = np.ones((P, SEQ), f), np.zeros((P, SEQ), f)
        for base in range(0, P - width + 1, width):
            for r in range(n_rot):
                row, partner = base + at + r, base + at + (r + half) % n_rot
                m[partner, row] = -1.0 if r < half else 1.0
                cc[row], ss[row] = np.cos(ang[:, r % half]), np.sin(ang[:, r % half])
        c[:, DCOL[rot]], c[:, DCOL[cos]], c[:, DCOL[sin]] = m, cc, ss

    rotary(16, 0, HD, "rot_p", "cos_p", "sin_p")
    rotary(MLA_ROPE, MLA_NOPE, MLA_QK, "rot_m", "cos_m", "sin_m")
    both = lambda m: m.T.reshape(2, P, SEQ).transpose(1, 0, 2).reshape(P, 2 * SEQ)
    c[:, DCOL["sb_add"]] = both(np.where(k < q, 0.0, MASKED))
    c[:, DCOL["sb_mul"]] = both(np.where(k < q, 1.0, 0.0))
    return con, b, c


def tiles(w):
    kk, n = w.shape
    return w.reshape(kk // P, P, n // P, P).transpose(2, 1, 0, 3)


def fm_chunks(w, order=None):
    t = tiles(w)
    if order is not None:
        t = t[order]
    n = t.shape[0] // 2
    return t.reshape(n, 2, P, KT, P).transpose(0, 2, 1, 3, 4).reshape(n, P, CH)


def tm_chunks(w):
    n = w.shape[1] // SEQ
    return w.reshape(KT, P, n, SEQ).transpose(2, 1, 0, 3).reshape(n, P, CH)


def down_chunks(w):
    n = w.shape[0] // (2 * P)
    return w.reshape(n, 2, P, KT, P).transpose(0, 2, 1, 3, 4).reshape(n, P, CH)


def branch_chunks(w):
    t = tiles(w)
    return t.reshape(2, 4, P, 4, P).transpose(0, 2, 1, 3, 4).reshape(2, P, CH)


def padded(w):
    out = np.zeros((1, P, CH), np.float32)
    out[0, :, :w.shape[1]] = w
    return out


def qkv_chunks(w):
    return [fm_chunks(w[:, :1024]), tm_chunks(w[:, 1024:])]


def vector(a):
    return a.reshape(-1, P).T


def pairs(n):
    return np.stack([np.arange(n), n + np.arange(n)], 1).reshape(-1)


def layouts(i):
    w = []
    win = i["w_in"][0]
    w += qkv_chunks(win[:, 0:1536]) + qkv_chunks(win[:, 1536:3072]) + [fm_chunks(win[:, 3072:])]
    w += [branch_chunks(i["w_branch_dil"][0]), branch_chunks(i["w_branch_na"][0]), fm_chunks(i["w_out"][0])]
    w += [fm_chunks(i["w_up"][0], pairs(FT)), down_chunks(i["w_down"][0])]
    for l in range(LAYERS):
        def ffn(s):
            g, u = i["ffn_w_gate_2"][l, s], i["ffn_w_up_2"][l, s]
            return [fm_chunks(np.concatenate([g, u], 1), pairs(FT)), down_chunks(i["ffn_w_down_2"][l, s])]
        win = i["mix_w_in_2"][l]
        w += ffn(0) + qkv_chunks(win[:, 0:1536]) + qkv_chunks(win[:, 1536:3072]) + [fm_chunks(win[:, 3072:3328])]
        lat = np.zeros((KT, P, 224), np.float32)
        lat[:, :, 0:128] = win[:, 3328:3456].reshape(KT, P, 128)
        lat[:, :, 192:224] = win[:, 3456:3488].reshape(KT, P, 32)
        w.append(padded(lat.transpose(1, 0, 2).reshape(P, -1)))
        w.append(padded(i["mla_w_uq_2"][l].reshape(2, P, 768).transpose(1, 0, 2).reshape(P, -1)))
        kv = i["mla_w_ukv_2"][l].reshape(P, HEADS, 128)
        up = np.zeros((P, HEADS, MLA_QK), np.float32)
        up[:, :, 0:64] = kv[:, :, 0:64]
        w.append(padded(np.concatenate([up.reshape(P, -1), kv[:, :, 64:].reshape(P, -1)], 1)))
        w.append(fm_chunks(win[:, 3488:]))
        w += [branch_chunks(i["mix_w_branch_2"][l, n]) for n in range(3)] + [fm_chunks(i["mix_w_out_2"][l])]
        w += ffn(1)
    w.append(np.zeros((SPLIT + RAW, P, CH), np.float32))
    ada = np.concatenate([fm_chunks(i["w_ada"][0])] + [fm_chunks(i["ada_w_2"][l]) for l in range(LAYERS)]
                         + [np.zeros((2, P, CH), np.float32)])

    par = np.zeros((P, NPCOL), np.float32)
    for name in ("c", "c_2", "b_ada", "g_mix", "g_ffn", "g_final"):
        par[:, PCOL[name]] = vector(i[name].reshape(-1))
    taps = np.concatenate([i["conv_w"][0], i["conv_b"]], 0)
    par[:, PCOL["conv"]] = taps.reshape(4, 2, FT, P).transpose(3, 2, 1, 0).reshape(P, -1)
    par[0:32, PCOL["rel_bias"]] = i["rel_bias"]
    lpar = np.zeros((LAYERS, P, NLCOL), np.float32)
    for l in range(LAYERS):
        for name, key in (("ada_b", "ada_b_2"), ("norm_pre", "norm_pre_2"), ("norm_post", "norm_post_2"),
                          ("b_gate", "mix_b_gate_2"), ("q_norm", "mla_q_norm_2"), ("kv_norm", "mla_kv_norm_2")):
            lpar[l][:, LCOL[name]] = vector(i[key][l].reshape(-1))
    con, bcon, dcon = constants()
    return {"w": np.concatenate(w), "ada": ada, "par": par, "lpar": lpar, "con": con, "bcon": bcon, "dcon": dcon,
            "x": np.ascontiguousarray(i["x"][0].T.reshape(KT, P, SEQ).transpose(1, 0, 2)),
            "rpb": np.ascontiguousarray(i["na_rpb"][0].reshape(HEADS, N_RPB))}


def tensors(nc, arrays):
    d = {n: nc.dram_tensor(f"in_{n}", a.shape, F32, kind="ExternalInput").ap() for n, a in arrays.items()}
    d["rel"] = nc.dram_tensor("rel_rows", [HEADS, 2 * SEQ], F32, kind="Internal").ap()
    d["out"] = nc.dram_tensor("out_x", [P, KT, SEQ], F32, kind="ExternalOutput").ap()
    return d


def kernel(**inputs):
    import concourse.bacc as bacc
    from concourse.bass_utils import run_bass_kernel_spmd

    arrays = layouts({n: np.asarray(a) for n, a in inputs.items()})
    draft = bacc.Bacc("TRN2", target_bir_lowering=False, num_devices=1)
    totals = program(draft, tensors(draft, arrays), {})
    nc = bacc.Bacc("TRN2", target_bir_lowering=False, num_devices=1)
    program(nc, tensors(nc, arrays), totals)
    r = run_bass_kernel_spmd(nc, [{f"in_{n}": a for n, a in arrays.items()}], core_ids=[0])
    out = r.results[0]["out_x"]
    return np.ascontiguousarray(out.transpose(2, 1, 0).reshape(1, SEQ, D))
```
